# Optimizing a Trainium2 kernel written in Bass

```python
import jax, jax.numpy as jnp
from jax import lax
import numpy as np

D_MODEL = 1024
BATCH = 1
SEQ = 512
DEPTH = 2
DEC_BATCH = 1
DEC_SEQ = 64
PAST_LEN = 256

CHUNK = 64
N_A = DEPTH // 2
N_B = DEPTH - N_A
POOL_WINDOWS = (2, 4, 8, 16)
POOL_GROUPS = len(POOL_WINDOWS)
POOL_WIDTH = D_MODEL // 2
POOL_GROUP_DIM = POOL_WIDTH // POOL_GROUPS
POOL_HIST = max(POOL_WINDOWS) - 1
FOX_HEAD_DIM = 64
FOX_WIDTH = D_MODEL // 2
FOX_HEADS = FOX_WIDTH // FOX_HEAD_DIM
MEM_TOKENS = 256
MEM_HEADS = 4
MEM_WIDTH = D_MODEL // 2
MEM_HEAD_DIM = MEM_WIDTH // MEM_HEADS
MIX_WIDTH = POOL_WIDTH + MEM_WIDTH
D_FF = ((8 * D_MODEL // 3 + 255) // 256) * 256
Q_BLOCK = 128
EPS = 1e-6
FORGET_BIAS_INIT = 3.0
FOX_SCALE = FOX_HEAD_DIM ** -0.5
MEM_SCALE = MEM_HEAD_DIM ** -0.5

kernel_name = 'yoco_pool_fox_stream_step'

def rmsnorm(x, g):
    xf = x.astype(jnp.float32)
    y = xf * lax.rsqrt(jnp.mean(xf * xf, axis=-1, keepdims=True) + EPS)
    return (y * g.astype(jnp.float32)).astype(x.dtype)

def pool_mix(u, hist, pos0, w_pool, scale):
    B, L, P = u.shape
    up = jnp.concatenate([hist.astype(u.dtype), u], axis=1).astype(jnp.float32)
    c = jnp.concatenate([jnp.zeros((B, 1, P), jnp.float32), jnp.cumsum(up, axis=1)], axis=1)
    end = c[:, POOL_HIST + 1:]
    pos = pos0 + jnp.arange(L)
    means = []
    for g, w in enumerate(POOL_WINDOWS):
        sl = slice(g * POOL_GROUP_DIM, (g + 1) * POOL_GROUP_DIM)
        start = c[:, POOL_HIST + 1 - w:POOL_HIST + 1 - w + L, sl]
        cnt = jnp.minimum(pos + 1, w).astype(jnp.float32)[None, :, None]
        means.append((end[..., sl] - start) / cnt)
    d = (jnp.concatenate(means, axis=-1) - up[:, POOL_HIST:]).reshape(B, L, POOL_GROUPS, POOL_GROUP_DIM)
    y = jnp.einsum('blgc,gcd->blgd', d, w_pool.astype(jnp.float32)).reshape(B, L, P)
    return (y * scale.astype(jnp.float32)).astype(u.dtype)

def mem_kv(mem, g_mem, w_mem_kv, k_norm_mem):
    B, M, _ = mem.shape
    kv = rmsnorm(mem, g_mem) @ w_mem_kv
    k = rmsnorm(kv[..., :MEM_WIDTH].reshape(B, M, MEM_HEADS, MEM_HEAD_DIM), k_norm_mem)
    v = kv[..., MEM_WIDTH:].reshape(B, M, MEM_HEADS, MEM_HEAD_DIM)
    return k, v

def mem_attend(q, k, v):
    s = jnp.einsum('blhd,bmhd->bhlm', q, k).astype(jnp.float32) * MEM_SCALE
    p = jax.nn.softmax(s, axis=-1).astype(v.dtype)
    return jnp.einsum('bhlm,bmhd->blhd', p, v)

def shared_kv(x, g_kv, w_kv, k_norm_fox, b_f):
    B, L, _ = x.shape
    z = rmsnorm(x, g_kv) @ w_kv
    k = rmsnorm(z[..., :FOX_WIDTH].reshape(B, L, FOX_HEADS, FOX_HEAD_DIM), k_norm_fox)
    v = z[..., FOX_WIDTH:2 * FOX_WIDTH].reshape(B, L, FOX_HEADS, FOX_HEAD_DIM)
    logf = jax.nn.log_sigmoid(z[..., 2 * FOX_WIDTH:].astype(jnp.float32) + b_f.astype(jnp.float32))
    return k, v, logf

def fox_attention(q, k, v, Fq, Fk, q_off):
    B, Lq, H, Dh = q.shape
    kpos = jnp.arange(k.shape[1])
    Fk_t = jnp.swapaxes(Fk, 1, 2)[:, :, None, :]

    def block(args):
        qb, fqb, qpos = args
        s = jnp.einsum('bqhd,bkhd->bhqk', qb, k).astype(jnp.float32) * FOX_SCALE
        s = s + jnp.swapaxes(fqb, 1, 2)[..., None] - Fk_t
        s = jnp.where(kpos[None, :] <= qpos[:, None], s, -jnp.inf)
        p = jax.nn.softmax(s, axis=-1).astype(v.dtype)
        return jnp.einsum('bhqk,bkhd->bqhd', p, v)

    qpos = q_off + jnp.arange(Lq)
    if Lq <= Q_BLOCK:
        return block((q, Fq, qpos))
    nb = Lq // Q_BLOCK
    qs = jnp.swapaxes(q.reshape(B, nb, Q_BLOCK, H, Dh), 0, 1)
    fs = jnp.swapaxes(Fq.reshape(B, nb, Q_BLOCK, H), 0, 1)
    out = lax.map(block, (qs, fs, qpos.reshape(nb, Q_BLOCK)))
    return jnp.swapaxes(out, 0, 1).reshape(B, Lq, H, Dh)

def swiglu(x, g, w_gu, w_down):
    gu = rmsnorm(x, g) @ w_gu
    return (jax.nn.silu(gu[..., :D_FF]) * gu[..., D_FF:]) @ w_down

def trunk(x, pos0, pool_hist, fox_past, mem_k, mem_v, g_mix, w_in, w_out, q_norm_mem,
          w_pool, pool_scale, q_norm_fox, g_kv, w_kv, k_norm_fox, b_f, g_ffn, w_gu, w_down):
    B, L, _ = x.shape
    pool_states = []
    fox_new = None
    for i in range(DEPTH):
        z = rmsnorm(x, g_mix[i]) @ w_in[i]
        qm = rmsnorm(z[..., MIX_WIDTH - MEM_WIDTH:].reshape(B, L, MEM_HEADS, MEM_HEAD_DIM), q_norm_mem[i])
        om = mem_attend(qm, mem_k[i].astype(x.dtype), mem_v[i].astype(x.dtype)).reshape(B, L, MEM_WIDTH)
        if i < N_A:
            u = z[..., :POOL_WIDTH]
            op = pool_mix(u, pool_hist[i], pos0, w_pool[i], pool_scale[i])
            pool_states.append(jnp.concatenate([pool_hist[i].astype(u.dtype), u], axis=1)[:, -POOL_HIST:])
        else:
            if i == N_A:
                k_new, v_new, lf_new = shared_kv(x, g_kv, w_kv, k_norm_fox, b_f)
                fox_new = (k_new, v_new, lf_new)
                if fox_past is None:
                    k_all, v_all, lf_all = k_new, v_new, lf_new
                else:
                    k_all = jnp.concatenate([fox_past[0].astype(k_new.dtype), k_new], axis=1)
                    v_all = jnp.concatenate([fox_past[1].astype(v_new.dtype), v_new], axis=1)
                    lf_all = jnp.concatenate([fox_past[2].astype(jnp.float32), lf_new], axis=1)
                F_all = jnp.cumsum(lf_all, axis=1)
                Fq = F_all[:, -L:]
                q_off = k_all.shape[1] - L
            qf = rmsnorm(z[..., :FOX_WIDTH].reshape(B, L, FOX_HEADS, FOX_HEAD_DIM), q_norm_fox[i - N_A])
            op = fox_attention(qf, k_all, v_all, Fq, F_all, q_off).reshape(B, L, FOX_WIDTH)
        x = x + jnp.concatenate([op, om], axis=-1) @ w_out[i]
        x = x + swiglu(x, g_ffn[i], w_gu[i], w_down[i])
    return x, jnp.stack(pool_states), fox_new

def setup_inputs(seed: int = 0) -> dict:
    key = jax.random.key(seed)
    ks = iter(jax.random.split(key, 40))
    D = D_MODEL

    def nrm(shape, scale=1.0):
        return scale * jax.random.normal(next(ks), shape, jnp.float32)

    def gain(shape):
        return 1.0 + nrm(shape, 0.05)

    inp = {}
    inp['x_prompt'] = nrm((BATCH, SEQ, D))
    inp['x_sample'] = nrm((DEC_BATCH, DEC_SEQ, D))
    inp['state_pool'] = nrm((N_A, DEC_BATCH, POOL_HIST, POOL_WIDTH))
    inp['cache_fox_k'] = nrm((DEC_BATCH, PAST_LEN, FOX_HEADS, FOX_HEAD_DIM))
    inp['cache_fox_v'] = nrm((DEC_BATCH, PAST_LEN, FOX_HEADS, FOX_HEAD_DIM))
    inp['cache_fox_logf'] = jax.nn.log_sigmoid(FORGET_BIAS_INIT + nrm((DEC_BATCH, PAST_LEN, FOX_HEADS)))
    inp['cache_mem_k'] = nrm((DEPTH, DEC_BATCH, MEM_TOKENS, MEM_HEADS, MEM_HEAD_DIM))
    inp['cache_mem_v'] = nrm((DEPTH, DEC_BATCH, MEM_TOKENS, MEM_HEADS, MEM_HEAD_DIM))
    inp['mem_prompt'] = nrm((BATCH, MEM_TOKENS, D))
    inp['g_mix'] = gain((DEPTH, D))
    inp['w_in'] = nrm((DEPTH, D, MIX_WIDTH), D ** -0.5)
    inp['w_out'] = nrm((DEPTH, MIX_WIDTH, D), MIX_WIDTH ** -0.5)
    inp['q_norm_mem'] = gain((DEPTH, MEM_HEAD_DIM))
    inp['g_mem'] = gain((DEPTH, D))
    inp['w_mem_kv'] = nrm((DEPTH, D, 2 * MEM_WIDTH), D ** -0.5)
    inp['k_norm_mem'] = gain((DEPTH, MEM_HEAD_DIM))
    inp['w_pool'] = nrm((N_A, POOL_GROUPS, POOL_GROUP_DIM, POOL_GROUP_DIM), POOL_GROUP_DIM ** -0.5)
    inp['pool_scale'] = 1.0 + nrm((N_A, POOL_WIDTH), 0.1)
    inp['q_norm_fox'] = gain((N_B, FOX_HEAD_DIM))
    inp['g_kv'] = gain((D,))
    inp['w_kv'] = nrm((D, 2 * FOX_WIDTH + FOX_HEADS), D ** -0.5)
    inp['k_norm_fox'] = gain((FOX_HEAD_DIM,))
    inp['b_f'] = FORGET_BIAS_INIT + nrm((FOX_HEADS,), 0.1)
    inp['g_ffn'] = gain((DEPTH, D))
    inp['w_gu'] = nrm((DEPTH, D, 2 * D_FF), D ** -0.5)
    inp['w_down'] = nrm((DEPTH, D_FF, D), D_FF ** -0.5)
    return inp

def reference(x_prompt, x_sample, state_pool, cache_fox_k, cache_fox_v, cache_fox_logf,
              cache_mem_k, cache_mem_v, mem_prompt, g_mix, w_in, w_out, q_norm_mem, g_mem,
              w_mem_kv, k_norm_mem, w_pool, pool_scale, q_norm_fox, g_kv, w_kv, k_norm_fox,
              b_f, g_ffn, w_gu, w_down):
    mks, mvs = [], []
    for i in range(DEPTH):
        mk, mv = mem_kv(mem_prompt, g_mem[i], w_mem_kv[i], k_norm_mem[i])
        mks.append(mk)
        mvs.append(mv)
    mem_k_prompt = jnp.stack(mks)
    mem_v_prompt = jnp.stack(mvs)
    pool_hist0 = jnp.zeros((N_A, x_prompt.shape[0], POOL_HIST, POOL_WIDTH), x_prompt.dtype)
    y_prompt, pool_state_prompt, fox_p = trunk(
        x_prompt, 0, pool_hist0, None, mem_k_prompt, mem_v_prompt, g_mix, w_in, w_out,
        q_norm_mem, w_pool, pool_scale, q_norm_fox, g_kv, w_kv, k_norm_fox, b_f, g_ffn, w_gu, w_down)
    y_sample, pool_state_sample, fox_s = trunk(
        x_sample, PAST_LEN, state_pool, (cache_fox_k, cache_fox_v, cache_fox_logf),
        cache_mem_k, cache_mem_v, g_mix, w_in, w_out, q_norm_mem, w_pool, pool_scale,
        q_norm_fox, g_kv, w_kv, k_norm_fox, b_f, g_ffn, w_gu, w_down)
    fox_k_prompt, fox_v_prompt, fox_logf_prompt = fox_p
    fox_k_sample, fox_v_sample, fox_logf_sample = fox_s
    return (y_prompt, y_sample, pool_state_prompt, fox_k_prompt, fox_v_prompt, fox_logf_prompt,
            mem_k_prompt, mem_v_prompt, pool_state_sample, fox_k_sample, fox_v_sample, fox_logf_sample)


_drawn_inputs = setup_inputs


def setup_inputs(seed=0):
    import zlib

    import numpy as np

    out = dict(_drawn_inputs(seed))
    spreads = {}
    factors = {'cache_fox_logf': 7.337, 'q_norm_mem': 8.0, 'q_norm_fox': 7.929}
    for name, (base, spread) in spreads.items():
        noise = np.random.default_rng([zlib.crc32(name.encode()), seed]).standard_normal(out[name].shape)
        drawn = base * np.exp(spread * noise) if base else spread * noise
        out[name] = __import__('jax').numpy.asarray(drawn.astype(out[name].dtype))
    for name, factor in factors.items():
        out[name] = (out[name] * factor).astype(out[name].dtype)
    return out
```

```python
from contextlib import ExitStack

import numpy as np

import concourse.bass as bass
from concourse import mybir

F32 = mybir.dt.float32
F32R = mybir.dt.float32r
BF16 = mybir.dt.bfloat16
ACT = mybir.ActivationFunctionType
ALU = mybir.AluOpType
AX = mybir.AxisListType

P = 128
EPS = 1e-6
WINDOWS = (2, 4, 8, 16)
NEG = -1.0e38
RAW_SLOTS = 4
SPLIT_SLOTS = 2


def at(base, per=0, i=0):
    if isinstance(i, int) or per == 0:
        return base + (per * i if per else 0)
    return i * per + base


class Step:

    def __init__(self, kind=None, p=None, g=None, view=None, ncol=None, moving=None, evac=None, c=None,
                 first=None, xs=None, layer=None, s=None, buf=None, width=None, m=None, n=None, gain=None,
                 block=None, name=None, t=None, o=None, jobs=None, ys=None, y=None, mh=None, r=None,
                 which=None, nsub=None, final=None, body=None, z=None, rjob=None, j=None, att=None, u=None,
                 h=None, e=None, per=None, nq=None, nk=None, last=None):
        self.kind = kind
        self.p = p
        self.g = g
        self.view = view
        self.ncol = ncol
        self.moving = moving
        self.evac = evac
        self.c = c
        self.first = first
        self.xs = xs
        self.layer = layer
        self.s = s
        self.buf = buf
        self.width = width
        self.m = m
        self.n = n
        self.gain = gain
        self.block = block
        self.name = name
        self.t = t
        self.o = o
        self.jobs = jobs
        self.ys = ys
        self.y = y
        self.mh = mh
        self.r = r
        self.which = which
        self.nsub = nsub
        self.final = final
        self.body = body
        self.z = z
        self.rjob = rjob
        self.j = j
        self.att = att
        self.u = u
        self.h = h
        self.e = e
        self.per = per
        self.nq = nq
        self.nk = nk
        self.last = last


def encoder_kernel(nc, ins, outs):
    x_prompt, x_sample = ins["x_prompt"], ins["x_sample"]
    D = x_prompt.shape[2]
    L = x_prompt.shape[1]
    LS = x_sample.shape[1]
    T = L + LS
    KC = D // P
    DEPTH = ins["w_in"].shape[0]
    FF = ins["w_down"].shape[1]
    FC = FF // P
    MT_TOK = ins["mem_prompt"].shape[1]
    MK = MT_TOK // P
    HIST = ins["state_pool"].shape[2]
    PAST = ins["cache_fox_k"].shape[1]
    PK = PAST // P
    FH = ins["cache_fox_k"].shape[2]
    FD = ins["cache_fox_k"].shape[3]
    W2 = D // 2
    HC = W2 // P
    HALF = T // 2
    TT = L // P
    NT = TT + 1
    assert L % P == 0 and LS == 64 and DEPTH == 2 and HC == 4 and FD == 64 and FC % 2 == 0
    assert TT == 4 and MK == 2 and PK == 2 and HALF <= 512
    SUB = [(FC + 3 - s) // 4 for s in range(4)]
    SUB0 = [sum(SUB[:s]) for s in range(4)]
    assert sum(SUB) == FC and max(SUB) <= KC

    steps = []
    count = {"panel": 0, "acc": 0, "job": 0, "sq": 0, "x": 0, "xs": 0, "ys": 0, "unit": 0,
             "normed": 0, "load": 0, "store": 0, "zero": 0, "r": 0, "silu": 0, "h": 0, "rm": 0, "pool": 0}
    panel_shape = []
    units_before, jobs_before, sq_before, sq_of_norm, rows_by_unit = {}, {}, {}, {}, {}
    branch_acc = {}

    def take(what, n=1):
        count[what] += n
        if what == "job":
            for m in range(count["job"] - n, count["job"]):
                units_before[m] = count["unit"]
        return count[what] - n

    def add(kind, **f):
        s = Step(kind=kind, **f)
        steps.append(s)
        return s

    def panel(view, nk, ncol=P):
        p = take("panel")
        panel_shape.append((nk, ncol))
        return p

    def group(view, ncol, moving, evac, **f):
        p = panel(view, KC, ncol)
        g = take("acc")
        add("group", p=p, g=g, view=view, ncol=ncol, moving=moving, **f)
        add("evac", p=p, g=g, evac=evac, **f)
        return g

    def square(buf, c, g, width):
        return add("square", s=take("sq"), buf=buf, c=c, g=g, width=width).s

    def norm(s, buf, c, gain, width, block):
        n = add("norm", s=s, m=take("job"), n=take("normed"), buf=buf, c=c, gain=gain,
                width=width, block=block, layer=layer).n
        sq_of_norm[n] = s
        return n

    def turn(name, **f):
        return add("turn", name=name, m=take("job"), **f).m

    def store(name, **f):
        return add("store", name=name, o=take("store"), **f).o

    def resid(layer, which, nsub, pbase):
        f = dict(layer=layer, which=which, nsub=nsub, p=pbase, g=take("acc", KC), o=count["store"],
                 final=layer == DEPTH - 1 and which == "down", body=4 if nsub == 1 else 2)
        if f["final"]:
            f.update(m=take("job", KC))
        else:
            f.update(xs=take("xs", KC), s=take("sq", KC), z=take("zero"), rjob=rjob[0])
        add("resid", **f)

    rjob = [0]
    marks = {}

    def colsof(w, n0, n1):
        return lambda: w[:, :, n0:n1]

    w_in = [ins["w_in"][i].rearrange("(k p) n -> p k n", p=P) for i in range(DEPTH)]
    w_out = [ins["w_out"][i].rearrange("(k p) n -> p k n", p=P) for i in range(DEPTH)]
    w_mem = [ins["w_mem_kv"][i].rearrange("(k p) n -> p k n", p=P) for i in range(DEPTH)]
    w_kv = ins["w_kv"].rearrange("(k p) n -> p k n", p=P)
    w_gu = [ins["w_gu"][i].rearrange("(k p) n -> p k n", p=P) for i in range(DEPTH)]
    w_down = [ins["w_down"][i].rearrange("(k p) n -> p k n", p=P) for i in range(DEPTH)]

    def attend(kind, layer, heads):
        units = [(h, t) for h in heads for t in range(NT)]
        u0 = take("unit", len(units))
        per = 1 if kind == "mem" else 2
        rows = []
        for n, (h, t) in enumerate(units):
            c = h // per
            if h % per == 0 and t == 0:
                g = take("acc")
                y = take("ys")
            keys = MT_TOK if kind == "mem" else (P * (t + 1) if t < TT else PAST + LS)
            rows_by_unit[u0 + n] = Step(kind="unit", att=kind, u=u0 + n, h=h, t=t, c=c, e=h % per, per=per,
                             nq=P if t < TT else LS, nk=keys, g=g, y=y,
                             first=n == 0, last=(h % per == per - 1 and t == NT - 1), layer=layer)
            rows.append(rows_by_unit[u0 + n])
            branch_acc[layer, c + (HC if kind == "mem" else 0)] = g
        jobs_before[u0], sq_before[u0] = count["job"], count["sq"]
        for n in range(len(rows) + 3):
            if n < len(rows):
                add("scores", r=rows[n])
            if 0 <= n - 2 < len(rows):
                add("turn_probs", r=rows[n - 2])
            if 0 <= n - 3 < len(rows):
                add("values", r=rows[n - 3])

    xsq_of = {}
    for layer in range(DEPTH):
        if layer == 0:
            turn("vectors")
            for t in range(NT):
                turn("x", t=t)
            for c in range(KC):
                square("x0", c, None, T)
                add("split_x0", c=c, xs=take("xs"), s=count["sq"] - 1)
            xsq_of[0] = count["sq"]
        add("load_mem", layer=layer, p=count["panel"])
        if layer == 0:
            for t in range(MK):
                turn("mem", t=t, layer=layer)
            add("mem_split", layer=layer, s=take("sq", KC), jobs=count["job"])
        order = list(range(HC, 2 * HC)) + list(range(HC))
        pend = []
        xsq = xsq_of[layer]
        for n, c in enumerate(order):
            kind = "q" if c >= HC else ("u" if layer == 0 else "fq")
            late = pend.pop(0) if n >= 2 and pend else None
            if late:
                s = square(late[0], late[1], late[2], T)
            g = group(colsof(w_in[layer], c * P, (c + 1) * P), P, "x", kind, c=c % HC,
                      first=n == 0, xs=layer * 2 * KC, layer=layer)
            if n == 0:
                rjob[0] = take("job")
                steps.insert(len(steps) - 1, Step(kind="r", m=rjob[0], r=take("r"), s=xsq))
            if n == 1 and layer == 1:
                for t in range(MK):
                    turn("mem", t=t, layer=layer)
                add("mem_split", layer=layer, s=take("sq", KC), jobs=count["job"])
            if kind != "u":
                pend.append((kind, c % HC, g))
            if late:
                norm(s, late[0], late[1], late[0], T, late[0] == "fq")
        if layer == 1:
            for c in range(KC):
                add("split_kv", c=c, ys=take("ys"))
        add("rm", m=take("job"), r=take("rm"))
        if layer == 0:
            marks["hist"] = turn("hist")
        heads = pend
        pend = []
        for c in range(2 * HC):
            kind = "mk" if c < HC else "mv"
            ready_ = [z for z in pend if z[0] == "mk" and z[3] <= c]
            late = heads.pop(0) + (T,) if heads else ((ready_[0][0], ready_[0][1], ready_[0][2], MT_TOK) if ready_ else None)
            if late:
                s = square(late[0], late[1], late[2], late[3])
            if ready_ and late[0] == "mk":
                pend.remove(ready_[0])
            g = group(colsof(w_mem[layer], c * P, (c + 1) * P), P, "m", kind, c=c % HC,
                      first=c == 0, xs=layer * KC, layer=layer)
            if layer == 0 and c >= 2 and c < 2 + HC:
                branch_acc[0, c - 2] = take("acc")
                add("pool", c=c - 2, g=branch_acc[0, c - 2], y=take("ys"), n=take("pool"))
            if late:
                n = norm(s, late[0], late[1], late[0], late[3], late[0] == "fq")
                if late[0] == "mk":
                    pend.append(("mkt", late[1], n, c + 1))
            for z in [z for z in pend if z[3] <= c and z[0] in ("mv", "mkt")]:
                if z[0] == "mv":
                    turn("mv", c=z[1], g=z[2], layer=layer)
                else:
                    turn("mk", c=z[1], n=z[2], layer=layer)
                pend.remove(z)
            pend.append((kind, c % HC, g, c + 1))
        assert not heads
        for kd, cc, gg, late in sorted(pend, key=lambda z: z[0] != "mk"):
            if kd == "mk":
                n = norm(square("mk", cc, gg, MT_TOK), "mk", cc, "mk", MT_TOK, False)
                turn("mk", c=cc, n=n, layer=layer)
            elif kd == "mv":
                turn("mv", c=cc, g=gg, layer=layer)
            else:
                turn("mk", c=cc, n=gg, layer=layer)
        mem_jobs = count["job"]
        store("mem", layer=layer, m=mem_jobs)
        add("load_caches", layer=layer, m=mem_jobs, p=count["panel"], mh=(layer + 1) * KC)
        turn("cmk", layer=layer)
        if layer == 0:
            turn("state")
            store("state", m=count["job"])
        else:
            pend = []
            for c in range(2 * HC + 1):
                kind = "fk" if c < HC else ("fv" if c < 2 * HC else "gate")
                early = [z for z in pend if z[0] == "fk" and z[3] <= c]
                if early:
                    s = square("fk", early[0][1], early[0][2], T)
                ncol = P if c < 2 * HC else FH
                g = group(colsof(w_kv, c * P, c * P + ncol), ncol, "y", kind, c=c % HC,
                          first=c == 0, xs=0, layer=layer)
                for z in [z for z in pend if z[3] <= c]:
                    kd, cc, gg, late = z
                    if kd == "fk":
                        n = norm(s, "fk", cc, "fk", T, True)
                        pend.append(("fkt", cc, n, c + 1))
                    elif kd == "fkt":
                        m = turn("fk", c=cc, n=gg, o=count["store"])
                        store("fk", c=cc, m=m)
                    elif kd == "fv":
                        turn("fv", c=cc, g=gg)
                    pend.remove(z)
                pend.append((kind, c % HC, g, c + 1))
            for kd, cc, gg, late in pend:
                if kd == "fv":
                    turn("fv", c=cc, g=gg)
                elif kd == "fkt":
                    m = turn("fk", c=cc, n=gg, o=count["store"])
                    store("fk", c=cc, m=m)
            store("fv", m=count["job"])
            turn("gate", g=g)
            add("log_sigmoid", m=count["job"])
            store("logf")
            turn("cfk")
            add("cumsum", m=take("job"))
            attend("fox", layer, range(FH))
        attend("mem", layer, range(HC))
        p = count["panel"]
        for n in range(KC):
            panel(None, KC)
        if layer == 0:
            assert count["ys"] == KC
        resid(layer, "out", 1, p)
        p = count["panel"]
        for n in range(2 * FC):
            panel(None, KC)
        add("up", layer=layer, p=p, g=take("acc", 2 * FC), j=take("h", FC), xs=layer * 2 * KC + KC,
            m=take("job"), r=take("r"), s=count["sq"])
        rjob[0] = count["job"] - 1
        p = count["panel"]
        for n in range(KC):
            for s in range(4):
                panel(None, SUB[s])
        resid(layer, "down", 4, p)
        xsq_of[layer + 1] = count["sq"]
    NPANEL = count["panel"]
    GATE_STEPS = 8
    F_STEPS = 7
    DVE_CONSTS = 6 + sum(w - 1 for w in WINDOWS)

    base = 16640
    ctx = ExitStack()
    with ctx:
        def place(name, shape, dt, offset):
            return nc.alloc_sbuf_tensor_at(name, shape, dt, offset=offset)

        XB = KC * T * 4
        o_x = base
        o_xh = o_x + XB
        o_hh = o_xh + 2 * XB
        o_hl = o_hh + FC * T * 4
        o_raw = o_hl + FC * T * 4
        o_wh = o_raw + RAW_SLOTS * KC * P * 4
        o_wl = o_wh + SPLIT_SLOTS * KC * P * 4
        o_e = o_wl + SPLIT_SLOTS * KC * P * 4
        X = place("X", [P, KC, T], F32, o_x)
        XH = place("XH", [P, KC, T], F32R, o_xh)
        XL = place("XL", [P, KC, T], F32R, o_xh + XB)
        HH = place("HH", [P, FC, T], F32R, o_hh)
        HL = place("HL", [P, FC, T], F32R, o_hl)
        RAW = place("RAW", [P, RAW_SLOTS, KC, P], F32, o_raw)
        WH = place("WH", [P, SPLIT_SLOTS, KC, P], F32R, o_wh)
        WL = place("WL", [P, SPLIT_SLOTS, KC, P], F32R, o_wl)

        top = [o_e]

        def small(name, shape, dt):
            size = 2 if dt == BF16 else 4
            for n in shape[1:]:
                size *= n
            size = (size + 31) // 32 * 32
            t = place(name, shape, dt, top[0])
            top[0] += size
            assert top[0] <= 229344, name
            return t

        R = small("R", [P, T], F32)
        RM = small("RM", [P, MT_TOK], F32)
        SQ = small("SQ", [P, 2, T], F32)
        ACC = small("ACC", [P, T], F32)
        TG = small("TG", [P, T], F32)
        TU = small("TU", [P, T], F32)
        TGU = [TG, TU]
        IDENT = small("IDENT", [P, P], F32)
        ONES = small("ONES", [P, P], F32)
        BLK = small("BLK", [P, P], F32)
        IDB = small("IDB", [P, P], BF16)
        MASK = small("MASK", [P, P], BF16)
        NVEC = 8 * 7 + 4 + HC + 2
        VROW = small("VROW", [NVEC, P], F32)
        VEC = small("VEC", [P, NVEC], F32)
        GQ = small("GQ", [P, 4], F32)
        BF = small("BF", [FH, 1], F32)
        EPSC = small("EPSC", [P, 2], F32)
        INVC = small("INVC", [P, HC, 16], F32)
        STAT = small("STAT", [P, 3, 4], F32)
        FP = small("FP", [96, L + PAST + LS], BF16)
        NFP = small("NFP", [96, L + PAST + LS], BF16)
        CL = small("CL", [P, PK, FH], F32)
        G_MIX, G_FFN, G_KV, G_MEM = 0, 16, 32, 40
        QN_M, KN_M, PSC, QN_F, KN_F = 56, 58, 60, 64, 65

        a0 = o_hh + XB
        b0 = o_hl + XB
        c0 = o_xh
        MB = KC * MT_TOK * 4
        MH = place("MH", [P, KC, MT_TOK], F32R, a0)
        ML = place("ML", [P, KC, MT_TOK], F32R, b0)
        MTR = place("MTR", [P, KC, MT_TOK], F32, a0 + MB)
        MRAW = place("MRAW", [P, MK, D], F32, b0 + MB)
        UW = HIST + L + HIST + LS
        U = place("U", [P, HC, UW], F32, a0 + 2 * MB)
        FQ = place("FQ", [P, HC, T], F32, a0 + 2 * MB)
        o_l3 = a0 + 2 * MB + HC * UW * 4
        L3 = place("L3", [P, NT + PK, 96], F32, o_l3)
        WP = place("WP", [P, HC, P], F32, o_l3)
        TRI = place("TRI", [P, L], F32, o_l3 + (NT + PK) * 96 * 4)
        assert o_l3 + (NT + PK) * 96 * 4 + L * 4 <= o_hl
        ZQ = place("ZQ", [P, HC, T], F32, b0 + 2 * MB)
        o_cfv = b0 + 2 * MB + HC * T * 4
        CFV = place("CFV", [P, PK, W2], F32, o_cfv)
        HRAW = place("HRAW", [HIST, W2], F32, o_cfv)
        SEL = place("SEL", [96, FH, P], BF16, o_cfv + PK * W2 * 4)
        assert o_cfv + PK * W2 * 4 + FH * P * 2 <= o_raw
        PR = place("PR", [P, 3, 512], F32, a0)
        FT = place("FT", [96, L + PAST + LS], F32, a0)
        PT = place("PT", [P, 2, 512], F32, b0)
        STG = [place("STG0", [P, NT, P], F32, b0 + MB + 4096), place("STG1", [P, NT, P], F32, b0 + 4096)]
        CMK = place("CMK", [P, MK, W2], F32, a0 + MB)
        CFK = place("CFK", [P, PK, W2], F32, a0 + MB + 4096)
        PST = place("PST", [HIST, 2, W2], F32, a0 + MB + 4096)
        CMV = place("CMV", [P, MK, W2], F32, b0 + MB)
        XR = place("XR", [P, TT, D], F32, o_hh)
        XRS = place("XRS", [LS, D], F32, o_hl)
        FK = place("FK", [P, HC, T], F32, c0)
        PW = place("PW", [P, 2, UW], F32, c0)
        o_vt = c0 + HC * T * 4
        VT = place("VT", [P, NT, W2], F32, o_vt)
        MKTOK = place("MKTOK", [P, MK, W2], F32, o_vt)
        PD = place("PD", [P, 2, T], F32, o_vt + 4096)
        o_c1 = o_vt + NT * W2 * 4
        CFKT = place("CFKT", [P, HC, PAST], F32, o_c1)
        MKT = place("MKT", [P, HC, MT_TOK], F32, o_c1 + 4096)
        MV = place("MV", [P, MK, W2], F32, o_c1 + 8192)
        CMKT = place("CMKT", [P, HC, MT_TOK], F32, o_c1 + 12288)
        YST = [place(f"YST{k}", [P, NT, P], F32, c0 + k * NT * P * 4) for k in range(2)]
        assert o_c1 + 16384 <= o_hh
        LG = small("LG", [P, 6, NT, FH], F32)

        ACCP = ctx.enter_context(nc.psum_tensor("ACCP", [P, 2, 2, 512], F32))
        MISC = ctx.enter_context(nc.psum_tensor("MISC", [P, 2, 2, 512], F32))

        def sem(name):
            return ctx.enter_context(nc.semaphore(name))

        raw_loaded = [sem(f"raw_loaded{i}") for i in range(RAW_SLOTS)]
        hi_ready, lo_ready = sem("hi_ready"), sem("lo_ready")
        panel_used, acc_free = sem("panel_used"), sem("acc_free")
        misc_done, misc_free = sem("misc_done"), sem("misc_free")
        sq_ready, sq_free = sem("sq_ready"), sem("sq_free")
        half_taken = sem("half_taken")
        xh_ready, xl_ready = sem("xh_ready"), sem("xl_ready")
        yh_ready, yl_ready = sem("yh_ready"), sem("yl_ready")
        mh_ready, ml_ready = sem("mh_ready"), sem("ml_ready")
        r_ready, rm_ready = sem("r_ready"), sem("rm_ready")
        ln_done = sem("ln_done")
        inv_ready, normed = sem("inv_ready"), sem("normed")
        silu_done, h_ready = sem("silu_done"), sem("h_ready")
        hh_ready, hl_ready = sem("hh_ready"), sem("hl_ready")
        scores_ready, max_ready, probs_ready = sem("scores_ready"), sem("max_ready"), sem("probs_ready")
        recip_ready, probs_normed = sem("recip_ready"), sem("probs_normed")
        probs_turned, pt_ready, pv_done = sem("probs_turned"), sem("pt_ready"), sem("pv_done")
        vec_loaded, mem_loaded, xin_loaded = sem("vec_loaded"), sem("mem_loaded"), [sem(f"xin{t}") for t in range(NT)]
        caches_loaded, hist_loaded, wp_loaded = sem("caches_loaded"), sem("hist_loaded"), sem("wp_loaded")
        fox_loaded, clf_loaded = sem("fox_loaded"), sem("clf_loaded")
        mem_stored, misc_stored = sem("mem_stored"), sem("misc_stored")
        fk_stored = [sem(f"fk_stored{k}") for k in range(2)]
        y_stored = [sem(f"y_stored{k}") for k in range(2)]
        consts, consts_dve = sem("consts"), sem("consts_dve")
        acc_zeroed = sem("acc_zeroed")
        window_done, pooled_in, pool_mm = sem("window_done"), sem("pooled_in"), sem("pool_mm")
        pads_ready = sem("pads_ready")
        gate_steps, gate_act = sem("gate_steps"), sem("gate_act")
        f_steps = sem("f_steps")
        sel_ready = sem("sel_ready")
        f_evac = sem("f_evac")

        block = ctx.enter_context(nc.Block())

        def halves(w):
            return [(0, w)] if w <= 512 and w != T else [(0, HALF), (HALF, T)]

        def moving_of(kind):
            return {"x": (XH, XL, xl_ready, T), "y": (HH, HL, yl_ready, T),
                    "m": (MH, ML, ml_ready, MT_TOK)}[kind]

        BUF = {"q": ZQ, "fq": FQ, "mk": MKT, "fk": FK}

        def r_scale(act, a, m, r):
            for k, (lo, hi) in enumerate(halves(T)):
                a.activation(R[:, lo:hi], MISC[:, m % 2, k, 0:hi - lo], ACT.Ln, bias=EPSC[:, 0:1], scale=1.0 / D)\
                    .then_inc(misc_free if k else ln_done, 1)
            act.wait_ge(misc_free, m + 1)
            a.activation(R[:], R[:], ACT.Exp, scale=-0.5).then_inc(r_ready, 1)

        def evac(s, dve, v):
            dve.wait_ge(panel_used, s.p + 1)
            ps = ACCP[:, s.g % 2]
            if s.evac in ("mk", "mv"):
                dve.wait_ge(rm_ready, s.layer + 1)
                dst = MKT[:, s.c] if s.evac == "mk" else TGU[s.c % 2][:, 0:MT_TOK]
                v.tensor_tensor(dst, ps[:, 0, 0:MT_TOK], RM[:], ALU.mult).then_inc(acc_free, 1)
                return
            dve.wait_ge(r_ready, 2 * s.layer + 1)
            if s.evac == "u":
                for dst, b, lo, hi, r0 in ((HIST, 0, 0, HALF, 0), (HIST + HALF, 1, 0, L - HALF, HALF),
                                           (2 * HIST + L, 1, L - HALF, HALF, L)):
                    v.tensor_tensor(U[:, s.c, dst:dst + hi - lo], ps[:, b, lo:hi], R[:, r0:r0 + hi - lo], ALU.mult)\
                        .then_inc(acc_free if r0 == L else half_taken, 1)
                return
            if s.evac == "gate":
                for b, (lo, hi) in enumerate(halves(T)):
                    v.tensor_tensor(TG[0:FH, lo:hi], ps[0:FH, b, 0:hi - lo], R[0:FH, lo:hi], ALU.mult).then_inc(f_evac, 1)
                dve.wait_ge(f_evac, 2)
                dve.wait_ge(clf_loaded, 32)
                v.tensor_scalar(TG[0:FH], TG[0:FH], BF[:, 0:1], None, ALU.add).then_inc(acc_free, 1)
                return
            dst = {"q": ZQ[:, s.c], "fq": FQ[:, s.c], "fk": FK[:, s.c], "fv": TGU[s.c % 2][:]}[s.evac]
            for b, (lo, hi) in enumerate(halves(T)):
                v.tensor_tensor(dst[:, lo:hi], ps[:, b, 0:hi - lo], R[:, lo:hi], ALU.mult)\
                    .then_inc(acc_free if b else half_taken, 1)

        def pool(s, dve, v):
            w = WINDOWS[s.c]
            done = window_base[s.c]
            dve.wait_ge(acc_free, s.g)
            dve.wait_ge(misc_free, marks["hist"] + 1)
            dve.wait_ge(pads_ready, 1)
            dve.wait_ge(consts_dve, DVE_CONSTS)
            sums = U[:, s.c]
            for n in range(s.c + 1):
                lo = 2 ** (n + 1) - 1
                if done:
                    dve.wait_ge(window_done, done)
                v.tensor_tensor(PW[:, n % 2, lo:UW], sums[:, lo:UW], sums[:, lo - 2 ** n:UW - 2 ** n], ALU.add).then_inc(window_done, 1)
                done += 1
                sums = PW[:, n % 2]
            if s.n >= 2:
                dve.wait_ge(pool_mm, s.n - 1)
            dve.wait_ge(window_done, done)
            d, u = PD[:, s.n % 2], U[:, s.c]
            q0, s0 = HIST, 2 * HIST + L
            v.scalar_tensor_tensor(d[:, w - 1:L], sums[:, q0 + w - 1:q0 + L], 1.0 / w, u[:, q0 + w - 1:q0 + L], ALU.mult, ALU.subtract).then_inc(window_done, 1)
            v.scalar_tensor_tensor(d[:, L:T], sums[:, s0:s0 + LS], 1.0 / w, u[:, s0:s0 + LS], ALU.mult, ALU.subtract).then_inc(window_done, 1)
            v.tensor_tensor(d[:, 0:w - 1], sums[:, q0:q0 + w - 1], INVC[:, s.c, 0:w - 1], ALU.mult).then_inc(window_done, 1)
            dve.wait_ge(window_done, done + 3)
            v.tensor_tensor(d[:, 0:w - 1], d[:, 0:w - 1], u[:, q0:q0 + w - 1], ALU.subtract).then_inc(pooled_in, 1)
            dve.wait_ge(yh_ready, s.y + 1)
            for b, (lo, hi) in enumerate(halves(T)):
                v.scalar_tensor_tensor(HL[:, s.c, lo:hi], ACCP[:, s.g % 2, b, 0:hi - lo], VEC[:, PSC + s.c:PSC + s.c + 1],
                                       HH[:, s.c, lo:hi], ALU.mult, ALU.subtract).then_inc(acc_free if b else half_taken, 1)

        window_base = [sum(g + 1 + 3 for g in range(c)) for c in range(HC)]

        def scale_probs(r, dve, v):
            dve.wait_ge(probs_ready, r.u + 1)
            v.reciprocal(STAT[0:r.nq, 2, r.u % 4:r.u % 4 + 1], STAT[0:r.nq, 1, r.u % 4:r.u % 4 + 1]).then_inc(recip_ready, 1)
            dve.wait_ge(recip_ready, r.u + 1)
            pr = PR[0:r.nq, r.u % 3, 0:r.nk]
            v.tensor_scalar(pr, pr, STAT[0:r.nq, 2, r.u % 4:r.u % 4 + 1], None, ALU.mult).then_inc(probs_normed, 1)

        @block.sync
        def _(sp):
            def load(p, src, per=0, i=0):
                nk, ncol = panel_shape[p]
                src = src if not callable(src) else src()
                if p >= RAW_SLOTS:
                    sp.wait_ge(lo_ready, at(p - RAW_SLOTS + 1, per, i))
                sp.dma_start(RAW[:, p % RAW_SLOTS, 0:nk, 0:ncol], src).then_inc(raw_loaded[p % RAW_SLOTS], 16)

            for s in steps:
                if s.kind == "group":
                    load(s.p, s.view)
                elif s.kind == "resid" and s.which == "out":
                    with sp.Fori(0, KC // 4) as i:
                        cols = [sp.snap(i * (4 * P) + k * P) for k in range(4)]
                        for k in range(4):
                            load(s.p + k, w_out[s.layer][:, :, bass.ds(cols[k], P)], 4, i)
                elif s.kind == "resid":
                    with sp.Fori(0, KC) as i:
                        col = sp.snap(i * P)
                        for k in range(4):
                            load(s.p + k, w_down[s.layer][:, SUB0[k]:SUB0[k] + SUB[k], bass.ds(col, P)], 4, i)
                elif s.kind == "up":
                    with sp.Fori(0, FC // 2) as i:
                        cols = [sp.snap(i * (2 * P) + (k // 2) * P + (k % 2) * FF) for k in range(4)]
                        for k in range(4):
                            load(s.p + k, w_gu[s.layer][:, :, bass.ds(cols[k], P)], 4, i)

        @block.gpsimd
        def _(gp):
            g = nc.gpsimd
            g.memset(IDENT[:], 0.0).then_inc(consts, 1)
            g.memset(IDB[:], 0.0).then_inc(consts, 1)
            g.memset(MASK[:], 0.0).then_inc(consts, 1)
            gp.wait_ge(consts, 3)
            g.affine_select(out=IDENT[:], in_=IDENT[:], compare_op=ALU.not_equal, fill=1.0, base=0,
                            pattern=[[-1, P]], channel_multiplier=1).then_inc(consts, 1)
            g.affine_select(out=IDB[:], in_=IDB[:], compare_op=ALU.not_equal, fill=1.0, base=0,
                            pattern=[[-1, P]], channel_multiplier=1).then_inc(consts, 1)
            g.affine_select(out=MASK[:], in_=MASK[:], compare_op=ALU.is_ge, fill=NEG, base=0,
                            pattern=[[-1, P]], channel_multiplier=1).then_inc(consts, 1)
            gp.dma_start(BF[:], ins["b_f"].rearrange("(h a) -> h a", a=1)).then_inc(clf_loaded, 16)
            gp.dma_start(CL[:], ins["cache_fox_logf"][0].rearrange("(t p) h -> p t h", p=P)).then_inc(clf_loaded, 16)
            gp.dma_start(WP[:], ins["w_pool"][0].rearrange("g c d -> c g d")).then_inc(wp_loaded, 16)
            gp.dma_start(HRAW[:], ins["state_pool"][0, 0]).then_inc(hist_loaded, 16)

            def out(dst, src, stored):
                gp.dma_start(dst, src).then_inc(stored, 16)

            for s in steps:
                if s.kind == "load_mem":
                    if s.p:
                        gp.wait_ge(panel_used, s.p)
                    gp.dma_start(MRAW[:], ins["mem_prompt"][0].rearrange("(t p) d -> p t d", p=P)).then_inc(mem_loaded, 16)
                    if s.layer == 1:
                        gp.wait_ge(misc_done, marks["hist"] + 1)
                        gp.dma_start(CFV[:], ins["cache_fox_v"][0].rearrange("(t p) h d -> p t (h d)", p=P)).then_inc(fox_loaded, 16)
                        g.memset(SEL[:], 0.0).then_inc(sel_ready, 1)
                        g.memset(TRI[:], 1.0).then_inc(sel_ready, 1)
                        gp.wait_ge(sel_ready, 2)
                        g.affine_select(out=TRI[:], in_=TRI[:], compare_op=ALU.is_ge, fill=0.0, base=0,
                                        pattern=[[1, L]], channel_multiplier=-1).then_inc(sel_ready, 1)
                        for j in range(3):
                            g.affine_select(out=SEL[:], in_=SEL[:], compare_op=ALU.not_equal, fill=1.0, base=-32 * j,
                                            pattern=[[-1, FH], [0, P]], channel_multiplier=1).then_inc(sel_ready, 1)
                            gp.wait_ge(sel_ready, 4 + j)
                elif s.kind == "load_caches":
                    gp.wait_ge(ml_ready, s.mh)
                    gp.wait_ge(misc_done, s.m)
                    gp.dma_start(CMK[:], ins["cache_mem_k"][s.layer, 0].rearrange("(t p) h d -> p t (h d)", p=P)).then_inc(caches_loaded, 16)
                    gp.dma_start(CMV[:], ins["cache_mem_v"][s.layer, 0].rearrange("(t p) h d -> p t (h d)", p=P)).then_inc(caches_loaded, 16)
                    if s.layer == 1:
                        gp.dma_start(CFK[:], ins["cache_fox_k"][0].rearrange("(t p) h d -> p t (h d)", p=P)).then_inc(fox_loaded, 16)
                elif s.kind == "store" and s.name == "mem":
                    gp.wait_ge(misc_free, s.m)
                    out(outs["mem_k_prompt"][s.layer, 0].rearrange("(t p) h d -> p t (h d)", p=P), MKTOK[:], mem_stored)
                    out(outs["mem_v_prompt"][s.layer, 0].rearrange("(t p) h d -> p t (h d)", p=P), MV[:], mem_stored)
                elif s.kind == "store" and s.name == "state":
                    gp.wait_ge(misc_free, s.m)
                    out(outs["pool_state_prompt"][0, 0], PST[:, 0], misc_stored)
                    out(outs["pool_state_sample"][0, 0], PST[:, 1], misc_stored)
                elif s.kind == "store" and s.name == "fk":
                    gp.wait_ge(misc_free, s.m + 1)
                    st = STG[s.c % 2]
                    out(outs["fox_k_prompt"][0].rearrange("(t p) h d -> p t (h d)", p=P)[:, :, s.c * P:(s.c + 1) * P], st[:, 0:TT], fk_stored[s.c % 2])
                    out(outs["fox_k_sample"][0].rearrange("t h d -> t (h d)")[:, s.c * P:(s.c + 1) * P], st[0:LS, TT], fk_stored[s.c % 2])
                elif s.kind == "store" and s.name == "fv":
                    gp.wait_ge(misc_free, s.m)
                    out(outs["fox_v_prompt"][0].rearrange("(t p) h d -> p t (h d)", p=P), VT[:, 0:TT], misc_stored)
                    out(outs["fox_v_sample"][0].rearrange("t h d -> t (h d)"), VT[0:LS, TT], misc_stored)
                elif s.kind == "store" and s.name == "logf":
                    gp.wait_ge(gate_steps, GATE_STEPS)
                    out(outs["fox_logf_prompt"][0].rearrange("(t p) h -> p t h", p=P), LG[:, 0, 0:TT], misc_stored)
                    out(outs["fox_logf_sample"][0], LG[0:LS, 0, TT], misc_stored)
                elif s.kind == "resid" and s.layer == DEPTH - 1 and s.which == "down":
                    yp = outs["y_prompt"][0].rearrange("(t p) d -> p t d", p=P)
                    with gp.Fori(0, KC // 2) as i:
                        for k in range(2):
                            col = gp.snap(i * (2 * P) + k * P)
                            gp.wait_ge(misc_free, at(s.m + k + 1, 2, i))
                            gp.dma_start(yp[:, :, bass.ds(col, P)], YST[k][:, 0:TT]).then_inc(y_stored[k], 16)
                            gp.dma_start(outs["y_sample"][0][:, bass.ds(col, P)], YST[k][0:LS, TT]).then_inc(y_stored[k], 16)
            gp.wait_ge(mem_stored, 32 * DEPTH)
            gp.wait_ge(misc_stored, 96)
            for k in range(2):
                gp.wait_ge(fk_stored[k], 16 * HC)
                gp.wait_ge(y_stored[k], 16 * KC)

        @block.scalar
        def _(act):
            a = nc.scalar
            act.dma_start(VROW[0:16], ins["g_mix"].rearrange("l (k p) -> (l k) p", p=P)).then_inc(vec_loaded, 16)
            act.dma_start(XR[:, 0], x_prompt[0, 0:P]).then_inc(xin_loaded[0], 16)
            act.dma_start(VROW[16:32], ins["g_ffn"].rearrange("l (k p) -> (l k) p", p=P)).then_inc(vec_loaded, 16)
            act.dma_start(VROW[32:40], ins["g_kv"].rearrange("(k p) -> k p", p=P)).then_inc(vec_loaded, 16)
            act.dma_start(VROW[40:56], ins["g_mem"].rearrange("l (k p) -> (l k) p", p=P)).then_inc(vec_loaded, 16)
            act.dma_start(VROW[QN_M:QN_M + 2], ins["q_norm_mem"]).then_inc(vec_loaded, 16)
            act.dma_start(VROW[KN_M:KN_M + 2], ins["k_norm_mem"]).then_inc(vec_loaded, 16)
            act.dma_start(VROW[PSC:PSC + HC], ins["pool_scale"].rearrange("l (k p) -> (l k) p", p=P)).then_inc(vec_loaded, 16)
            for e in range(2):
                act.dma_start(VROW[QN_F:QN_F + 1, e * FD:(e + 1) * FD], ins["q_norm_fox"]).then_inc(vec_loaded, 16)
                act.dma_start(VROW[KN_F:KN_F + 1, e * FD:(e + 1) * FD], ins["k_norm_fox"].rearrange("(a d) -> a d", a=1)).then_inc(vec_loaded, 16)
            for t in range(1, TT):
                act.dma_start(XR[:, t], x_prompt[0, t * P:(t + 1) * P]).then_inc(xin_loaded[t], 16)
            act.dma_start(XRS[:], x_sample[0]).then_inc(xin_loaded[TT], 16)

            def split_hi(q, per=0, i=0):
                if q >= NPANEL:
                    return
                nk, ncol = panel_shape[q]
                act.wait_ge(raw_loaded[q % RAW_SLOTS], at(16 * (q // RAW_SLOTS + 1), 4 * per, i))
                if q >= SPLIT_SLOTS:
                    act.wait_ge(panel_used, at(q - SPLIT_SLOTS + 1, per, i))
                a.activation(WH[:, q % SPLIT_SLOTS, 0:nk, 0:ncol], RAW[:, q % RAW_SLOTS, 0:nk, 0:ncol],
                             ACT.Copy).then_inc(hi_ready, 1)

            a.preload_act_table_set("natural_log_exp_and_others")
            split_hi(0)
            split_hi(1)
            for s in steps:
                if s.kind == "group":
                    split_hi(s.p + 2)
                elif s.kind == "turn":
                    act.wait_ge(misc_done, s.m + 1)
                    ps = MISC[:, s.m % 2]
                    if s.name == "vectors":
                        a.activation(VEC[:], ps[:, 0, 0:NVEC], ACT.Copy).then_inc(misc_free, 1)
                        act.wait_ge(misc_free, s.m + 1)
                        a.activation(GQ[:, 0:2], VEC[:, QN_M:QN_M + 2], ACT.Copy, scale=float(P) ** -0.5).then_inc(gate_act, 1)
                        a.activation(GQ[:, 2:3], VEC[:, QN_F:QN_F + 1], ACT.Copy, scale=float(FD) ** -0.5).then_inc(gate_act, 1)
                    elif s.name == "x":
                        n = P if s.t < TT else LS
                        src = ps[:, :, :].rearrange("p b (k t) -> p (b k) t", t=P)[:, :, 0:n]
                        a.activation(X[:, :, s.t * P:s.t * P + n], src, ACT.Copy).then_inc(misc_free, 1)
                    elif s.name == "mem":
                        src = ps[:, :, :].rearrange("p b (k t) -> p (b k) t", t=P)
                        a.activation(MTR[:, :, s.t * P:(s.t + 1) * P], src, ACT.Copy).then_inc(misc_free, 1)
                    elif s.name == "hist":
                        src = ps[:, 0, 0:HC * 16].rearrange("p (k t) -> p k t", t=16)[:, :, 0:HIST]
                        a.activation(U[:, :, HIST + L:2 * HIST + L], src, ACT.Copy).then_inc(misc_free, 1)
                    elif s.name == "mk":
                        a.activation(MKTOK[:, :, s.c * P:(s.c + 1) * P],
                                     ps[:, 0, 0:MT_TOK].rearrange("p (t c) -> p t c", c=P), ACT.Copy).then_inc(misc_free, 1)
                    elif s.name == "mv":
                        a.activation(MV[:, :, s.c * P:(s.c + 1) * P],
                                     ps[:, 0, 0:MT_TOK].rearrange("p (t c) -> p t c", c=P), ACT.Copy).then_inc(misc_free, 1)
                    elif s.name in ("cmk", "cfk"):
                        dst = CMKT if s.name == "cmk" else CFKT
                        a.activation(dst[:], ps.rearrange("p b (k t) -> p (b k) t", t=2 * P), ACT.Copy).then_inc(misc_free, 1)
                    elif s.name == "state":
                        a.activation(PST[:], ps[0:HIST], ACT.Copy).then_inc(misc_free, 1)
                    elif s.name == "fk":
                        if s.c >= 2:
                            act.wait_ge(fk_stored[s.c % 2], 32)
                        st = STG[s.c % 2]
                        a.activation(st[:, 0:TT], ps[:, 0].rearrange("p (t c) -> p t c", c=P), ACT.Copy).then_inc(ln_done, 1)
                        a.activation(st[0:LS, TT], ps[0:LS, 1, 0:P], ACT.Copy).then_inc(misc_free, 1)
                    elif s.name == "fv":
                        if s.c == 0:
                            act.wait_ge(mem_stored, 32 * DEPTH)
                        a.activation(VT[:, 0:TT, s.c * P:(s.c + 1) * P], ps[:, 0].rearrange("p (t c) -> p t c", c=P), ACT.Copy).then_inc(ln_done, 1)
                        a.activation(VT[0:LS, TT, s.c * P:(s.c + 1) * P], ps[0:LS, 1, 0:P], ACT.Copy).then_inc(misc_free, 1)
                    elif s.name == "gate":
                        act.wait_ge(consts_dve, DVE_CONSTS)
                        a.activation(LG[:, 1, 0:TT], ps[:, 0, 0:TT * FH].rearrange("p (t h) -> p t h", h=FH), ACT.Copy).then_inc(ln_done, 1)
                        a.activation(LG[0:LS, 1, TT], ps[0:LS, 0, TT * FH:NT * FH], ACT.Copy).then_inc(misc_free, 1)
                elif s.kind == "square":
                    if s.g is not None:
                        act.wait_ge(acc_free, s.g + 1)
                        src = BUF[s.buf][:, s.c]
                    else:
                        act.wait_ge(misc_free, NT + 1)
                        src = X[:, s.c]
                    if s.s >= 2:
                        act.wait_ge(sq_free, s.s - 1)
                    a.activation(SQ[:, s.s % 2, 0:s.width], src, ACT.Square).then_inc(sq_ready, 1)
                elif s.kind == "split_x0":
                    a.activation(XH[:, s.c], X[:, s.c], ACT.Copy, scale=VEC[:, G_MIX + s.c:G_MIX + s.c + 1]).then_inc(xh_ready, 1)
                elif s.kind == "split_kv":
                    a.activation(HH[:, s.c], X[:, s.c], ACT.Copy, scale=VEC[:, G_KV + s.c:G_KV + s.c + 1]).then_inc(yh_ready, 1)
                elif s.kind == "mem_split":
                    act.wait_ge(misc_free, s.jobs)
                    for c in range(KC):
                        q = s.s + c
                        if q >= 2:
                            act.wait_ge(sq_free, q - 1)
                        a.activation(SQ[:, q % 2, 0:MT_TOK], MTR[:, c], ACT.Square).then_inc(sq_ready, 1)
                        v = G_MEM + KC * s.layer + c
                        a.activation(MH[:, c], MTR[:, c], ACT.Copy, scale=VEC[:, v:v + 1]).then_inc(mh_ready, 1)
                elif s.kind in ("r", "rm"):
                    act.wait_ge(misc_done, s.m + 1)
                    if s.kind == "r":
                        r_scale(act, a, s.m, s.r)
                    else:
                        a.activation(RM[:], MISC[:, s.m % 2, 0, 0:MT_TOK], ACT.Ln, bias=EPSC[:, 0:1], scale=1.0 / D).then_inc(misc_free, 1)
                        act.wait_ge(misc_free, s.m + 1)
                        a.activation(RM[:], RM[:], ACT.Exp, scale=-0.5).then_inc(rm_ready, 1)
                elif s.kind == "norm":
                    act.wait_ge(misc_done, s.m + 1)
                    n = FD if s.block else P
                    hv = halves(s.width)
                    for k, (lo, hi) in enumerate(hv):
                        a.activation(SQ[:, s.s % 2, lo:hi], MISC[:, s.m % 2, k, 0:hi - lo], ACT.Ln, bias=EPSC[:, 0:1], scale=1.0 / n)\
                            .then_inc(misc_free if k == len(hv) - 1 else ln_done, 1)
                    act.wait_ge(misc_free, s.m + 1)
                    a.activation(SQ[:, s.s % 2, 0:s.width], SQ[:, s.s % 2, 0:s.width], ACT.Exp, scale=-0.5).then_inc(inv_ready, 1)
                elif s.kind == "pool":
                    act.wait_ge(pool_mm, s.n + 1)
                    for k, (lo, hi) in enumerate(halves(T)):
                        a.activation(HH[:, s.c, lo:hi], ACCP[:, s.g % 2, k, 0:hi - lo], ACT.Copy, scale=VEC[:, PSC + s.c:PSC + s.c + 1])\
                            .then_inc(yh_ready if k else ln_done, 1)
                elif s.kind == "log_sigmoid":
                    act.wait_ge(gate_steps, 1)
                    a.activation(LG[:, 3], LG[:, 2], ACT.Exp, scale=-1.0).then_inc(gate_act, 1)
                    act.wait_ge(gate_steps, 2)
                    a.activation(LG[:, 5], LG[:, 4], ACT.Ln).then_inc(gate_act, 1)
                elif s.kind == "cumsum":
                    act.wait_ge(misc_done, s.m + 1)
                    a.activation(FT[:, 0:L], MISC[0:96, s.m % 2, 0], ACT.Copy).then_inc(ln_done, 1)
                    a.activation(FT[:, L:], MISC[0:96, s.m % 2, 1, 0:PAST + LS], ACT.Copy).then_inc(misc_free, 1)
                elif s.kind == "scores":
                    r = s.r
                    act.wait_ge(max_ready, r.u + 1)
                    if r.u >= 3:
                        act.wait_ge(probs_turned, r.u - 2)
                    if r.first and r.att == "fox":
                        act.wait_ge(f_steps, F_STEPS)
                    a.activation(PR[0:r.nq, r.u % 3, 0:r.nk], MISC[0:r.nq, 0, r.u % 2, 0:r.nk], ACT.Exp,
                                 bias=STAT[0:r.nq, 0, r.u % 4:r.u % 4 + 1],
                                 accum_out=STAT[0:r.nq, 1, r.u % 4:r.u % 4 + 1]).then_inc(probs_ready, 1)
                elif s.kind == "turn_probs":
                    r = s.r
                    act.wait_ge(probs_turned, r.u + 1)
                    if r.u >= 2:
                        act.wait_ge(pv_done, r.u - 1)
                    ps = MISC[:, 1, r.u % 2].rearrange("p (k q) -> p k q", q=P)
                    pt = PT[:, r.u % 2].rearrange("p (k q) -> p k q", q=P)
                    full = r.nk // P
                    rest = r.nk % P
                    a.activation(pt[:, 0:full, 0:r.nq], ps[:, 0:full, 0:r.nq], ACT.Copy).then_inc(ln_done if rest else pt_ready, 1)
                    if rest:
                        a.activation(pt[0:rest, full, 0:r.nq], ps[0:rest, full, 0:r.nq], ACT.Copy).then_inc(pt_ready, 1)
                elif s.kind == "values" and s.r.last:
                    r = s.r
                    act.wait_ge(pv_done, r.u + 1)
                    c = r.c + (HC if r.att == "mem" else 0)
                    a.activation(HH[:, c, 0:L], ACCP[:, r.g % 2, 0, 0:L], ACT.Copy).then_inc(ln_done, 1)
                    a.activation(HH[:, c, L:T], ACCP[:, r.g % 2, 1, 0:LS], ACT.Copy).then_inc(yh_ready, 1)
                elif s.kind == "resid":
                    gain = (G_FFN + KC * s.layer) if s.which == "out" else (G_MIX + KC)
                    if s.which == "out":
                        act.wait_ge(mem_stored, 32 * (s.layer + 1))
                        act.wait_ge(misc_stored, 32 if s.layer == 0 else 96)
                        if s.layer == 1:
                            act.wait_ge(fk_stored[0], 16 * HC)
                            act.wait_ge(fk_stored[1], 16 * HC)

                    def take_y(k, turn_, i, s=s):
                        act.wait_ge(misc_done, at(s.m + turn_ + 1, s.body, i))
                        if turn_ >= 0:
                            if not isinstance(i, int) or i or turn_ > 1:
                                act.wait_ge(y_stored[k], at(32 * (turn_ // 2), 32, i))
                        elif not isinstance(i, int) or i > 1:
                            act.wait_ge(y_stored[k], at(-32, 32, i))
                        ps = MISC[:, (s.m + turn_) % 2]
                        a.activation(YST[k][:, 0:TT], ps[:, 0].rearrange("p (t c) -> p t c", c=P), ACT.Copy).then_inc(ln_done, 1)
                        a.activation(YST[k][0:LS, TT], ps[0:LS, 1, 0:P], ACT.Copy).then_inc(misc_free, 1)

                    def body(i, last, s=s, gain=gain):
                        nb, ns = s.body, s.nsub
                        for k in range(nb):
                            for q in range(ns):
                                if last:
                                    split_hi(s.p + (nb * i + k) * ns + q + 2)
                                else:
                                    split_hi(s.p + k * ns + q + 2, nb * ns, i)
                            if s.final:
                                if k or not isinstance(i, int) or i:
                                    take_y(1 - k, k - 1, i)
                                continue
                            n = i * nb + k
                            act.wait_ge(acc_free, at(s.g + k + 1, nb, i))
                            act.wait_ge(sq_free, at(s.s + k - 1, nb, i))
                            a.activation(SQ[:, (s.s + k) % 2], X[:, n], ACT.Square).then_inc(sq_ready, 1)
                            a.activation(XH[:, n], X[:, n], ACT.Copy, scale=VEC[:, bass.ds(n + gain, 1)]).then_inc(xh_ready, 1)

                    turns = KC // s.body
                    if s.final:
                        body(0, False)
                        body(1, False)
                    with act.Fori(2 if s.final else 0, turns if s.which == "out" else turns - 1) as i:
                        body(i, False)
                    if s.which == "down":
                        body(turns - 1, True)
                    if s.final:
                        take_y(1, KC - 1, 0)
                elif s.kind == "up":
                    def up_body(i, first, last, s=s):
                        for k in range(4):
                            if last:
                                split_hi(s.p + 4 * i + k + 2)
                            else:
                                split_hi(s.p + k + 2, 4, i)
                            if first and k == 0:
                                act.wait_ge(misc_done, s.m + 1)
                                r_scale(act, a, s.m, s.r)
                                a.preload_act_table_set("silu_and_others")
                            j = i * 2 + k // 2
                            if k % 2 == 0:
                                act.wait_ge(acc_free, at(s.g + k + 1, 4, i))
                                a.activation(TG[:], TG[:], ACT.Silu).then_inc(silu_done, 1)
                            else:
                                act.wait_ge(h_ready, at(s.j + k // 2 + 1, 2, i))
                                a.activation(HH[:, j], TU[:], ACT.Copy).then_inc(hh_ready, 1)
                    up_body(0, True, False)
                    with act.Fori(1, FC // 2 - 1) as i:
                        up_body(i, False, False)
                    up_body(FC // 2 - 1, False, True)
                    a.preload_act_table_set("natural_log_exp_and_others")

        @block.vector
        def _(dve):
            v = nc.vector
            v.memset(ONES[:], 1.0).then_inc(consts_dve, 1)
            v.memset(BLK[:], 0.0).then_inc(consts_dve, 1)
            v.memset(EPSC[:], EPS).then_inc(consts_dve, 1)
            v.memset(LG[:], 0.0).then_inc(consts_dve, 1)
            dve.wait_ge(consts_dve, 2)
            v.memset(BLK[0:FD, 0:FD], 1.0).then_inc(consts_dve, 1)
            v.memset(BLK[FD:P, FD:P], 1.0).then_inc(consts_dve, 1)
            for gi, w in enumerate(WINDOWS):
                for t in range(w - 1):
                    v.memset(INVC[:, gi, t:t + 1], 1.0 / (t + 1)).then_inc(consts_dve, 1)
            v.memset(U[:, :, 0:HIST], 0.0).then_inc(pads_ready, 1)

            def split_lo(q, per=0, i=0):
                if q >= NPANEL:
                    return
                nk, ncol = panel_shape[q]
                dve.wait_ge(hi_ready, at(q + 1, per, i))
                v.tensor_tensor(WL[:, q % SPLIT_SLOTS, 0:nk, 0:ncol], RAW[:, q % RAW_SLOTS, 0:nk, 0:ncol],
                                WH[:, q % SPLIT_SLOTS, 0:nk, 0:ncol], ALU.subtract).then_inc(lo_ready, 1)

            def split_lo_x(dst, x, gain, hi):
                return v.scalar_tensor_tensor(dst, x, gain, hi, ALU.mult, ALU.subtract)

            def sum_squares(q, width, first, acc, per=0, i=0):
                dve.wait_ge(sq_ready, at(q + 1, per, i))
                if first:
                    return v.tensor_copy(acc, SQ[:, q % 2, 0:width]).then_inc(sq_free, 1)
                dve.wait_ge(sq_free, at(q, per, i))
                return v.tensor_tensor(acc, acc, SQ[:, q % 2, 0:width], ALU.add).then_inc(sq_free, 1)

            split_lo(0)
            split_lo(1)
            for s in steps:
                if s.kind == "group":
                    split_lo(s.p + 2)
                elif s.kind == "square" and s.g is None:
                    sum_squares(s.s, T, s.c == 0, ACC[:])
                elif s.kind == "split_x0":
                    dve.wait_ge(xh_ready, s.xs + 1)
                    split_lo_x(XL[:, s.c], X[:, s.c], VEC[:, G_MIX + s.c:G_MIX + s.c + 1], XH[:, s.c]).then_inc(xl_ready, 1)
                elif s.kind == "split_kv":
                    dve.wait_ge(yh_ready, s.ys + 1)
                    split_lo_x(HL[:, s.c], X[:, s.c], VEC[:, G_KV + s.c:G_KV + s.c + 1], HH[:, s.c]).then_inc(yl_ready, 1)
                elif s.kind == "mem_split":
                    for c in range(KC):
                        sum_squares(s.s + c, MT_TOK, c == 0, TG[:, 0:MT_TOK])
                        dve.wait_ge(mh_ready, KC * s.layer + c + 1)
                        vv = G_MEM + KC * s.layer + c
                        split_lo_x(ML[:, c], MTR[:, c], VEC[:, vv:vv + 1], MH[:, c]).then_inc(ml_ready, 1)
                elif s.kind == "norm":
                    dve.wait_ge(inv_ready, s.n + 1)
                    gain = {"q": GQ[:, s.layer:s.layer + 1], "fq": GQ[:, 2:3],
                            "mk": VEC[:, KN_M + s.layer:KN_M + s.layer + 1], "fk": VEC[:, KN_F:KN_F + 1]}[s.gain]
                    b = BUF[s.buf][:, s.c]
                    if s.n == 0:
                        dve.wait_ge(gate_act, 2)
                    v.scalar_tensor_tensor(b, b, gain, SQ[:, s.s % 2, 0:s.width], ALU.mult, ALU.mult).then_inc(sq_free, 1)
                elif s.kind == "evac":
                    evac(s, dve, v)
                elif s.kind == "pool":
                    pool(s, dve, v)
                elif s.kind == "log_sigmoid":
                    dve.wait_ge(misc_free, s.m)
                    y = LG[:, 1]
                    v.scalar_tensor_tensor(LG[:, 2], y, -1.0, y, ALU.mult, ALU.max).then_inc(gate_steps, 1)
                    dve.wait_ge(gate_act, 3)
                    v.tensor_scalar(LG[:, 4], LG[:, 3], 1.0, None, ALU.add).then_inc(gate_steps, 1)
                    dve.wait_ge(gate_steps, 2)
                    v.scalar_tensor_tensor(LG[:, 3], LG[:, 4], -1.0, LG[:, 3], ALU.add, ALU.subtract).then_inc(gate_steps, 1)
                    v.reciprocal(LG[:, 2], LG[:, 4]).then_inc(gate_steps, 1)
                    dve.wait_ge(gate_steps, 4)
                    v.tensor_tensor(LG[:, 2], LG[:, 2], LG[:, 3], ALU.mult).then_inc(gate_steps, 1)
                    dve.wait_ge(gate_act, 4)
                    dve.wait_ge(gate_steps, 5)
                    v.tensor_tensor(LG[:, 5], LG[:, 5], LG[:, 2], ALU.subtract).then_inc(gate_steps, 1)
                    dve.wait_ge(gate_steps, 6)
                    v.scalar_tensor_tensor(LG[:, 0], y, 0.0, LG[:, 5], ALU.min, ALU.subtract).then_inc(gate_steps, 1)
                    v.memset(L3[:], 0.0).then_inc(gate_steps, 1)
                    dve.wait_ge(gate_steps, GATE_STEPS)
                    dve.wait_ge(clf_loaded, 32)
                    for j in range(3):
                        v.tensor_copy(L3[:, 0:NT, 32 * j:32 * j + FH], LG[:, 0]).then_inc(gate_steps, 1)
                        v.tensor_copy(L3[:, NT:NT + PK, 32 * j:32 * j + FH], CL[:]).then_inc(gate_steps, 1)
                elif s.kind == "cumsum":
                    dve.wait_ge(misc_free, s.m + 1)
                    n = [0]

                    def link(ins):
                        n[0] += 1
                        ins.then_inc(f_steps, 1)
                        dve.wait_ge(f_steps, n[0])
                    link(v.tensor_copy(FP[:], FT[:]))
                    link(v.tensor_tensor(FT[:], FT[:], FP[:], ALU.subtract))
                    for q0 in (32, 64):
                        link(v.tensor_copy(FP[q0:q0 + 32], FT[q0:q0 + 32]))
                    link(v.tensor_tensor(FT[64:96], FT[64:96], FP[64:96], ALU.subtract))
                    link(v.tensor_copy(FP[64:96], FT[64:96]))
                    link(v.tensor_scalar(NFP[:], FP[:], -1.0, None, ALU.mult))
                    assert n[0] == F_STEPS
                elif s.kind == "scores":
                    r = s.r
                    dve.wait_ge(scores_ready, r.u + 1)
                    if r.u >= 4:
                        dve.wait_ge(probs_normed, r.u - 3)
                        dve.wait_ge(probs_ready, r.u - 3)
                    v.tensor_reduce(STAT[0:r.nq, 0, r.u % 4:r.u % 4 + 1], MISC[0:r.nq, 0, r.u % 2, 0:r.nk],
                                    AX.X, ALU.max, negate=True).then_inc(max_ready, 1)
                    if not r.first:
                        scale_probs(rows_by_unit[r.u - 1], dve, v)
                    if r.u + 1 not in rows_by_unit or rows_by_unit[r.u + 1].first:
                        scale_probs(r, dve, v)
                elif s.kind == "values" and s.r.last:
                    r = s.r
                    c = r.c + (HC if r.att == "mem" else 0)
                    dve.wait_ge(yh_ready, r.y + 1)
                    v.tensor_tensor(HL[:, c, 0:L], ACCP[:, r.g % 2, 0, 0:L], HH[:, c, 0:L], ALU.subtract).then_inc(half_taken, 1)
                    v.tensor_tensor(HL[:, c, L:T], ACCP[:, r.g % 2, 1, 0:LS], HH[:, c, L:T], ALU.subtract).then_inc(acc_free, 1)
                elif s.kind == "resid":
                    gain = (G_FFN + KC * s.layer) if s.which == "out" else (G_MIX + KC)

                    def body(i, last, s=s, gain=gain):
                        nb, ns = s.body, s.nsub
                        for k in range(nb):
                            for q in range(ns):
                                if last:
                                    split_lo(s.p + (nb * i + k) * ns + q + 2)
                                else:
                                    split_lo(s.p + k * ns + q + 2, nb * ns, i)
                            n = i * nb + k
                            dve.wait_ge(panel_used, at(s.p + (k + 1) * ns, nb * ns, i))
                            if s.final:
                                dve.wait_ge(misc_done, at(s.m + k - 1, nb, i))
                            for hf, (lo, hi) in enumerate(halves(T)):
                                d = TGU[k][:, lo:hi] if s.final else X[:, n, lo:hi]
                                v.tensor_tensor(d, X[:, n, lo:hi], ACCP[:, (s.g + k) % 2, hf, 0:hi - lo],
                                                ALU.add).then_inc(acc_free if hf else half_taken, 1)
                            if s.final:
                                continue
                            sum_squares(s.s + k, T, False, ACC[:], nb, i)
                            dve.wait_ge(xh_ready, at(s.xs + k + 1, nb, i))
                            split_lo_x(XL[:, n], X[:, n], VEC[:, bass.ds(n + gain, 1)], XH[:, n]).then_inc(xl_ready, 1)

                    if not s.final:
                        dve.wait_ge(misc_done, s.rjob + 1)
                        v.memset(ACC[:], 0.0).then_inc(acc_zeroed, 1)
                        dve.wait_ge(acc_zeroed, s.z + 1)
                    turns = KC // s.body
                    with dve.Fori(0, turns if s.which == "out" else turns - 1) as i:
                        body(i, False)
                    if s.which == "down":
                        body(turns - 1, True)
                elif s.kind == "up":
                    def up_body(i, first, last, s=s):
                        for k in range(4):
                            if last:
                                split_lo(s.p + 4 * i + k + 2)
                            else:
                                split_lo(s.p + k + 2, 4, i)
                            if first and k == 0:
                                dve.wait_ge(r_ready, s.r + 1)
                            j = i * 2 + k // 2
                            dve.wait_ge(panel_used, at(s.p + k + 1, 4, i))
                            dst = TG if k % 2 == 0 else TU
                            for hf, (lo, hi) in enumerate(halves(T)):
                                v.tensor_tensor(dst[:, lo:hi], ACCP[:, (s.g + k) % 2, hf, 0:hi - lo], R[:, lo:hi],
                                                ALU.mult).then_inc(acc_free if hf else half_taken, 1)
                            if k % 2:
                                dve.wait_ge(acc_free, at(s.g + k + 1, 4, i))
                                dve.wait_ge(silu_done, at(s.j + k // 2 + 1, 2, i))
                                v.tensor_tensor(TU[:], TG[:], TU[:], ALU.mult).then_inc(h_ready, 1)
                                dve.wait_ge(hh_ready, at(s.j + k // 2 + 1, 2, i))
                                v.tensor_tensor(HL[:, j], TU[:], HH[:, j], ALU.subtract).then_inc(hl_ready, 1)
                    up_body(0, True, False)
                    with dve.Fori(1, FC // 2 - 1) as i:
                        up_body(i, False, False)
                    up_body(FC // 2 - 1, False, True)

        @block.tensor
        def _(pe):
            t = nc.tensor

            def product(p, g, nk, ncol, hi, lo, width, k0, first, last, per=0, i=0, ready=None):
                pe.wait_ge(lo_ready, at(p + 1, per, i))
                q = p % SPLIT_SLOTS
                hv = halves(width)
                for k in range(nk):
                    if ready is not None:
                        pe.wait_ge(*ready[k])
                    for n, (w, m) in enumerate(((WH, hi), (WH, lo), (WL, hi))):
                        for b, (c0_, c1_) in enumerate(hv):
                            done = last and k == nk - 1 and n == 2
                            ins_ = t.matmul(ACCP[0:ncol, g % 2, b, 0:c1_ - c0_], w[:, q, k, 0:ncol], m[:, k0 + k, c0_:c1_],
                                            start=first and k == 0 and n == 0, stop=done)
                ins_.then_inc(panel_used, 1)

            def misc_ready(m, per=0, i=0):
                if m >= 2 or per:
                    pe.wait_ge(misc_free, at(m - 1, per, i))
                if units_before.get(m, 0):
                    pe.wait_ge(probs_ready, units_before[m])
                    pe.wait_ge(pt_ready, units_before[m])

            def turn_blocks(m, blocks):
                for k, (dst, src, n) in enumerate(blocks):
                    last = t.transpose(dst, src, IDENT[0:n, 0:n])
                last.then_inc(misc_done, 1)

            def sums(m, mat, src, width, waits):
                hv = halves(width)
                for k, (lo, hi) in enumerate(hv):
                    last = t.matmul(MISC[:, m % 2, k, 0:hi - lo], mat[:], src[:, lo:hi], start=True, stop=True)
                last.then_inc(misc_done, 1)

            pe.wait_ge(consts, 6)
            pe.wait_ge(consts_dve, DVE_CONSTS)
            for s in steps:
                if s.kind == "group":
                    hi, lo, sem_, width = moving_of(s.moving)
                    if s.g >= 2:
                        pe.wait_ge(acc_free, s.g - 1)
                    product(s.p, s.g, KC, s.ncol, hi, lo, width, 0, True, True, ready=[(sem_, s.xs + k + 1) for k in range(KC)] if s.first else None)
                elif s.kind == "turn":
                    misc_ready(s.m)
                    ps = MISC[:, s.m % 2]
                    if s.name == "vectors":
                        pe.wait_ge(vec_loaded, 16 * 11)
                        turn_blocks(s.m, [(ps[:, 0, 0:NVEC], VROW[:], NVEC)])
                    elif s.name == "x":
                        pe.wait_ge(xin_loaded[s.t], 16)
                        n = P if s.t < TT else LS
                        src = XR[:, s.t] if s.t < TT else XRS[:]
                        turn_blocks(s.m, [(ps[:, k // 4, (k % 4) * P:(k % 4) * P + n], src[:, k * P:(k + 1) * P], n) for k in range(KC)])
                    elif s.name == "mem":
                        pe.wait_ge(mem_loaded, 16 * (s.layer + 1))
                        turn_blocks(s.m, [(ps[:, k // 4, (k % 4) * P:(k % 4 + 1) * P], MRAW[:, s.t, k * P:(k + 1) * P], P) for k in range(KC)])
                    elif s.name == "hist":
                        pe.wait_ge(hist_loaded, 16)
                        turn_blocks(s.m, [(ps[:, 0, 16 * k:16 * k + HIST], HRAW[:, k * P:(k + 1) * P], HIST) for k in range(HC)])
                    elif s.name == "mk":
                        pe.wait_ge(sq_free, sq_of_norm[s.n] + 1)
                        turn_blocks(s.m, [(ps[:, 0, k * P:(k + 1) * P], MKT[:, s.c, k * P:(k + 1) * P], P) for k in range(MK)])
                    elif s.name == "mv":
                        pe.wait_ge(acc_free, s.g + 1)
                        turn_blocks(s.m, [(ps[:, 0, k * P:(k + 1) * P], TGU[s.c % 2][:, k * P:(k + 1) * P], P) for k in range(MK)])
                    elif s.name == "cmk":
                        pe.wait_ge(caches_loaded, 32 * (s.layer + 1))
                        turn_blocks(s.m, [(ps[:, h // 2, (h % 2) * 256 + k * P:(h % 2) * 256 + (k + 1) * P], CMK[:, k, h * P:(h + 1) * P], P)
                                          for h in range(HC) for k in range(MK)])
                    elif s.name == "cfk":
                        pe.wait_ge(fox_loaded, 32)
                        turn_blocks(s.m, [(ps[:, h // 2, (h % 2) * 256 + k * P:(h % 2) * 256 + (k + 1) * P], CFK[:, k, h * P:(h + 1) * P], P)
                                          for h in range(HC) for k in range(PK)])
                    elif s.name == "state":
                        blocks = []
                        for w in range(2):
                            c_ = L if w == 0 else HIST + L + LS
                            blocks += [(ps[0:HIST, w, k * P:(k + 1) * P], U[:, k, c_:c_ + HIST], P) for k in range(HC)]
                        turn_blocks(s.m, blocks)
                    elif s.name in ("fk", "fv"):
                        if s.name == "fk":
                            pe.wait_ge(sq_free, sq_of_norm[s.n] + 1)
                            src = FK[:, s.c]
                        else:
                            pe.wait_ge(acc_free, s.g + 1)
                            src = TGU[s.c % 2][:]
                        turn_blocks(s.m, [(ps[:, 0, k * P:(k + 1) * P], src[:, k * P:(k + 1) * P], P) for k in range(TT)]
                                    + [(ps[0:LS, 1, 0:P], src[:, L:T], P)])
                    elif s.name == "gate":
                        pe.wait_ge(acc_free, s.g + 1)
                        turn_blocks(s.m, [(ps[:, 0, k * FH:(k + 1) * FH], TG[0:FH, k * P:(k + 1) * P], FH) for k in range(TT)]
                                    + [(ps[0:LS, 0, TT * FH:NT * FH], TG[0:FH, L:T], FH)])
                elif s.kind == "r":
                    misc_ready(s.m)
                    pe.wait_ge(sq_free, s.s)
                    sums(s.m, ONES, ACC, T, None)
                elif s.kind == "rm":
                    misc_ready(s.m)
                    pe.wait_ge(ml_ready, KC * (s.r + 1))
                    sums(s.m, ONES, TG, MT_TOK, None)
                elif s.kind == "norm":
                    misc_ready(s.m)
                    pe.wait_ge(sq_ready, s.s + 1)
                    sums(s.m, BLK if s.block else ONES, SQ[:, s.s % 2], s.width, None)
                elif s.kind == "pool":
                    pe.wait_ge(pooled_in, s.n + 1)
                    pe.wait_ge(wp_loaded, 16)
                    pe.wait_ge(acc_free, s.g - 1)
                    for k, (lo, hi) in enumerate(halves(T)):
                        last = t.matmul(ACCP[:, s.g % 2, k, 0:hi - lo], WP[:, s.c], PD[:, s.n % 2, lo:hi], start=True, stop=True)
                    last.then_inc(pool_mm, 1)
                elif s.kind == "cumsum":
                    misc_ready(s.m)
                    pe.wait_ge(gate_steps, GATE_STEPS + 6)
                    pe.wait_ge(sel_ready, 6)
                    for k in range(TT):
                        t.matmul(MISC[0:96, s.m % 2, 0, k * P:L], L3[:, k], TRI[:, 0:L - k * P], start=k == 0, stop=k == TT - 1)
                    n = PAST + LS
                    for k in range(PK):
                        t.matmul(MISC[0:96, s.m % 2, 1, k * P:n], L3[:, NT + k], TRI[:, 0:n - k * P], start=k == 0, stop=False)
                    t.matmul(MISC[0:96, s.m % 2, 1, PAST:n], L3[0:LS, TT], TRI[0:LS, 0:LS], start=False, stop=True).then_inc(misc_done, 1)
                elif s.kind == "scores":
                    r = s.r
                    if r.first:
                        pe.wait_ge(misc_free, jobs_before[r.u])
                        pe.wait_ge(sq_free, sq_before[r.u])
                        if r.layer == 1:
                            pe.wait_ge(f_steps, F_STEPS)
                    if r.u >= 2:
                        pe.wait_ge(probs_ready, r.u - 1)
                    q0 = r.t * P
                    S = MISC[0:r.nq, 0, r.u % 2]
                    if r.att == "mem":
                        kt = MKT if r.t < TT else CMKT
                        last = t.matmul(S[:, 0:r.nk], ZQ[:, r.h, q0:q0 + r.nq], kt[:, r.h], start=True, stop=True)
                    else:
                        rows = slice(r.e * FD, (r.e + 1) * FD)
                        q = FQ[rows, r.c, q0:q0 + r.nq]
                        if r.t < TT:
                            t.matmul(S[:, 0:r.nk], q, FK[rows, r.c, 0:r.nk], start=True, stop=False)
                            f0 = 0
                        else:
                            t.matmul(S[:, 0:PAST], q, CFKT[rows, r.c], start=True, stop=False)
                            t.matmul(S[:, PAST:PAST + LS], q, FK[rows, r.c, L:T], start=False, stop=False)
                            f0 = L
                        fq = r.t * P if r.t < TT else L + PAST
                        for k in range(0, r.nk, P):
                            n = min(P, r.nk - k)
                            t.matmul(S[:, k:k + n], FP[:, fq:fq + r.nq], SEL[:, r.h, 0:n], start=False, stop=False)
                        t.matmul(S[:, 0:r.nk], SEL[:, r.h, 0:r.nq], NFP[:, f0:f0 + r.nk], start=False, stop=False)
                        last = t.matmul(S[:, r.nk - r.nq:r.nk], IDB[:, 0:r.nq], MASK[:, 0:r.nq], start=False, stop=True)
                    last.then_inc(scores_ready, 1)
                elif s.kind == "turn_probs":
                    r = s.r
                    pe.wait_ge(probs_normed, r.u + 1)
                    if r.u >= 2:
                        pe.wait_ge(pt_ready, r.u - 1)
                    for k in range(0, r.nk, P):
                        n = min(P, r.nk - k)
                        last = t.transpose(MISC[0:n, 1, r.u % 2, k:k + r.nq], PR[0:r.nq, r.u % 3, k:k + n], IDENT[0:r.nq, 0:r.nq])
                    last.then_inc(probs_turned, 1)
                elif s.kind == "values":
                    r = s.r
                    pe.wait_ge(pt_ready, r.u + 1)
                    if r.t == 0 and r.e == 0:
                        pe.wait_ge(acc_free, r.g - 1)
                    if r.att == "mem":
                        vt = MV if r.t < TT else CMV
                        tiles = [(vt[:, k, r.h * P:(r.h + 1) * P], P) for k in range(MK)]
                        rows = slice(0, P)
                    else:
                        cols = slice(r.h * FD, (r.h + 1) * FD)
                        if r.t < TT:
                            tiles = [(VT[:, k, cols], P) for k in range(r.t + 1)]
                        else:
                            tiles = [(CFV[:, k, cols], P) for k in range(PK)] + [(VT[0:LS, TT, cols], LS)]
                        rows = slice(r.e * FD, (r.e + 1) * FD)
                    o = ACCP[rows, r.g % 2, 0, r.t * P:(r.t + 1) * P] if r.t < TT else ACCP[rows, r.g % 2, 1, 0:LS]
                    for k, (vk, n) in enumerate(tiles):
                        last = t.matmul(o, vk, PT[0:n, r.u % 2, k * P:k * P + r.nq], start=k == 0, stop=k == len(tiles) - 1)
                    last.then_inc(pv_done, 1)
                elif s.kind == "resid":
                    if s.which == "down":
                        ready = [(hl_ready, s.layer * FC + k + 1) for k in range(FC)]
                    else:
                        ready = [(acc_free, branch_acc[s.layer, k] + 1) for k in range(KC)]

                    def y_turn(k, turn_, i, s=s):
                        m = s.m + turn_
                        misc_ready(m, s.body, i)
                        pe.wait_ge(acc_free, at(s.g + turn_ + 1, s.body, i))
                        ps = MISC[:, m % 2]
                        turn_blocks(m, [(ps[:, 0, b * P:(b + 1) * P], TGU[k][:, b * P:(b + 1) * P], P) for b in range(TT)]
                                    + [(ps[0:LS, 1, 0:P], TGU[k][:, L:T], P)])

                    def body(i, first, s=s, ready=ready):
                        nb, ns = s.body, s.nsub
                        for k in range(nb):
                            pe.wait_ge(acc_free, at(s.g + k - 1, nb, i))
                            for q in range(ns):
                                nk = KC if ns == 1 else SUB[q]
                                k0 = 0 if ns == 1 else SUB0[q]
                                product(s.p + k * ns + q, s.g + k, nk, P, HH, HL, T, k0, q == 0, q == ns - 1,
                                        nb * ns, i, ready[k0:k0 + nk] if first and k == 0 else None)
                            if s.final and (k or not first):
                                y_turn(1 - k, k - 1, i)

                    body(0, True)
                    with pe.Fori(1, KC // s.body) as i:
                        body(i, False)
                    if s.final:
                        y_turn(1, KC - 1, 0)
                elif s.kind == "up":
                    def up_body(i, first, s=s):
                        for k in range(4):
                            pe.wait_ge(acc_free, at(s.g + k - 1, 4, i))
                            product(s.p + k, s.g + k, KC, P, XH, XL, T, 0, True, True, 4, i,
                                    [(xl_ready, s.xs + c + 1) for c in range(KC)] if first and k == 0 else None)
                            if first and k == 0:
                                misc_ready(s.m)
                                pe.wait_ge(sq_free, s.s)
                                sums(s.m, ONES, ACC, T, None)
                    up_body(0, True)
                    with pe.Fori(1, FC // 2) as i:
                        up_body(i, False)


_INS = ["x_prompt", "x_sample", "state_pool", "cache_fox_k", "cache_fox_v", "cache_fox_logf", "cache_mem_k",
        "cache_mem_v", "mem_prompt", "g_mix", "w_in", "w_out", "q_norm_mem", "g_mem", "w_mem_kv", "k_norm_mem",
        "w_pool", "pool_scale", "q_norm_fox", "g_kv", "w_kv", "k_norm_fox", "b_f", "g_ffn", "w_gu", "w_down"]


def kernel(**inputs):
    import concourse.bacc as bacc
    from concourse.bass_utils import run_bass_kernel_spmd

    B, L, D = inputs["x_prompt"].shape
    DB, LS, _ = inputs["x_sample"].shape
    NA, _, HIST, PW = inputs["state_pool"].shape
    _, _, FH, FD = inputs["cache_fox_k"].shape
    DEPTH, _, M, MHEADS, MD = inputs["cache_mem_k"].shape
    shapes = {
        "y_prompt": (B, L, D), "y_sample": (DB, LS, D), "pool_state_prompt": (NA, B, HIST, PW),
        "fox_k_prompt": (B, L, FH, FD), "fox_v_prompt": (B, L, FH, FD), "fox_logf_prompt": (B, L, FH),
        "mem_k_prompt": (DEPTH, B, M, MHEADS, MD), "mem_v_prompt": (DEPTH, B, M, MHEADS, MD),
        "pool_state_sample": (NA, DB, HIST, PW),
        "fox_k_sample": (DB, LS, FH, FD), "fox_v_sample": (DB, LS, FH, FD), "fox_logf_sample": (DB, LS, FH),
    }
    nc = bacc.Bacc("TRN2", target_bir_lowering=False, num_devices=1)
    arrays, ins = {}, {}
    for name in _INS:
        a = np.ascontiguousarray(inputs[name])
        arrays[f"in_{name}"] = a
        ins[name] = nc.dram_tensor(f"in_{name}", a.shape, mybir.dt.from_np(a.dtype), kind="ExternalInput").ap()
    outs = {name: nc.dram_tensor(f"out_{name}", shape, F32, kind="ExternalOutput").ap() for name, shape in shapes.items()}
    encoder_kernel(nc, ins, outs)
    r = run_bass_kernel_spmd(nc, [arrays], core_ids=[0])
    return tuple(r.results[0][f"out_{name}"] for name in shapes)
```

```python
from contextlib import ExitStack

import numpy as np

import concourse.bass as bass
from concourse import mybir

F32 = mybir.dt.float32
F32R = mybir.dt.float32r
BF16 = mybir.dt.bfloat16
ACT = mybir.ActivationFunctionType
ALU = mybir.AluOpType
AX = mybir.AxisListType

P = 128
EPS = 1e-6
WINDOWS = (2, 4, 8, 16)
NEG = -1.0e38
RAW_SLOTS = 4
SPLIT_SLOTS = 2


def at(base, per=0, i=0):
    if isinstance(i, int) or per == 0:
        return base + (per * i if per else 0)
    return i * per + base


class Step:

    def __init__(self, kind=None, p=None, g=None, view=None, ncol=None, moving=None, evac=None, c=None,
                 first=None, xs=None, layer=None, s=None, buf=None, width=None, m=None, n=None, gain=None,
                 block=None, name=None, t=None, o=None, jobs=None, ys=None, y=None, mh=None, r=None,
                 which=None, nsub=None, final=None, body=None, z=None, rjob=None, j=None, att=None, u=None,
                 h=None, e=None, per=None, nq=None, nk=None, last=None):
        self.kind = kind
        self.p = p
        self.g = g
        self.view = view
        self.ncol = ncol
        self.moving = moving
        self.evac = evac
        self.c = c
        self.first = first
        self.xs = xs
        self.layer = layer
        self.s = s
        self.buf = buf
        self.width = width
        self.m = m
        self.n = n
        self.gain = gain
        self.block = block
        self.name = name
        self.t = t
        self.o = o
        self.jobs = jobs
        self.ys = ys
        self.y = y
        self.mh = mh
        self.r = r
        self.which = which
        self.nsub = nsub
        self.final = final
        self.body = body
        self.z = z
        self.rjob = rjob
        self.j = j
        self.att = att
        self.u = u
        self.h = h
        self.e = e
        self.per = per
        self.nq = nq
        self.nk = nk
        self.last = last


def encoder_kernel(nc, ins, outs):
    x_prompt, x_sample = ins["x_prompt"], ins["x_sample"]
    D = x_prompt.shape[2]
    L = x_prompt.shape[1]
    LS = x_sample.shape[1]
    T = L + LS
    KC = D // P
    DEPTH = ins["w_in"].shape[0]
    FF = ins["w_down"].shape[1]
    FC = FF // P
    MT_TOK = ins["mem_prompt"].shape[1]
    MK = MT_TOK // P
    HIST = ins["state_pool"].shape[2]
    PAST = ins["cache_fox_k"].shape[1]
    PK = PAST // P
    FH = ins["cache_fox_k"].shape[2]
    FD = ins["cache_fox_k"].shape[3]
    W2 = D // 2
    HC = W2 // P
    HALF = T // 2
    TT = L // P
    NT = TT + 1
    assert L % P == 0 and LS == 64 and DEPTH == 2 and HC == 4 and FD == 64 and FC % 2 == 0
    assert TT == 4 and MK == 2 and PK == 2 and HALF <= 512
    SUB = [(FC + 3 - s) // 4 for s in range(4)]
    SUB0 = [sum(SUB[:s]) for s in range(4)]
    assert sum(SUB) == FC and max(SUB) <= KC

    steps = []
    count = {"panel": 0, "acc": 0, "job": 0, "sq": 0, "xs": 0, "ys": 0, "unit": 0, "normed": 0, "store": 0,
             "zero": 0, "win": 0, "r": 0, "h": 0, "rm": 0, "msq": 0, "pool": 0}
    panel_shape = []
    units_before, jobs_before, sq_before, sq_of_norm, rows_by_unit = {}, {}, {}, {}, {}
    branch_acc = {}

    def take(what, n=1):
        count[what] += n
        if what == "job":
            for m in range(count["job"] - n, count["job"]):
                units_before[m] = count["unit"]
        return count[what] - n

    def add(kind, **f):
        s = Step(kind=kind, **f)
        steps.append(s)
        return s

    def panel(view, nk, ncol=P):
        p = take("panel")
        panel_shape.append((nk, ncol))
        return p

    def group(view, ncol, moving, evac, **f):
        p = panel(view, KC, ncol)
        g = take("acc")
        add("group", p=p, g=g, view=view, ncol=ncol, moving=moving, **f)
        add("evac", p=p, g=g, evac=evac, **f)
        return g

    def square(buf, c, g, width):
        return add("square", s=take("sq"), buf=buf, c=c, g=g, width=width).s

    def norm(s, buf, c, gain, width, block):
        n = add("norm", s=s, m=take("job"), n=take("normed"), buf=buf, c=c, gain=gain,
                width=width, block=block, layer=layer).n
        sq_of_norm[n] = s
        return n

    def turn(name, **f):
        return add("turn", name=name, m=take("job"), **f).m

    def store(name, **f):
        return add("store", name=name, o=take("store"), **f).o

    def resid(layer, which, nsub, pbase):
        f = dict(layer=layer, which=which, nsub=nsub, p=pbase, g=take("acc", KC), o=count["store"],
                 final=layer == DEPTH - 1 and which == "down", body=4 if nsub == 1 else 2)
        if f["final"]:
            f.update(m=take("job", KC))
        else:
            f.update(xs=take("xs", KC), s=take("sq", KC), z=take("zero"), rjob=rjob[0])
        add("resid", **f)

    rjob = [0]
    marks = {}

    def colsof(w, n0, n1):
        return lambda: w[:, :, n0:n1]

    w_in = [ins["w_in"][i].rearrange("(k p) n -> p k n", p=P) for i in range(DEPTH)]
    w_out = [ins["w_out"][i].rearrange("(k p) n -> p k n", p=P) for i in range(DEPTH)]
    w_mem = [ins["w_mem_kv"][i].rearrange("(k p) n -> p k n", p=P) for i in range(DEPTH)]
    w_kv = ins["w_kv"].rearrange("(k p) n -> p k n", p=P)
    w_gu = [ins["w_gu"][i].rearrange("(k p) n -> p k n", p=P) for i in range(DEPTH)]
    w_down = [ins["w_down"][i].rearrange("(k p) n -> p k n", p=P) for i in range(DEPTH)]

    def attend(layer, branches):
        units = [(kind, h, t) for kind, heads in branches for h in heads for t in range(NT)]
        u0 = take("unit", len(units))
        rows = []
        for n, (kind, h, t) in enumerate(units):
            per = 1 if kind == "mem" else 2
            c = h // per
            if h % per == 0 and t == 0:
                g = take("acc")
                y = take("ys")
            keys = MT_TOK if kind == "mem" else (P * (t + 1) if t < TT else PAST + LS)
            rows_by_unit[u0 + n] = Step(kind="unit", att=kind, u=u0 + n, h=h, t=t, c=c, e=h % per, per=per,
                                        nq=P if t < TT else LS, nk=keys, g=g, y=y, first=n == 0,
                                        last=(h % per == per - 1 and t == NT - 1), layer=layer)
            rows.append(rows_by_unit[u0 + n])
            branch_acc[layer, c + (HC if kind == "mem" else 0)] = g
        jobs_before[u0], sq_before[u0] = count["job"], count["sq"]
        for n in range(len(rows) + 5):
            if n < len(rows):
                add("scores", r=rows[n])
            if 0 <= n - 2 < len(rows):
                add("turn_probs", r=rows[n - 2])
            if n < len(rows):
                add("exp", r=rows[n])
            if 0 <= n - 3 < len(rows):
                add("values", r=rows[n - 3])
            if 0 <= n - 4 < len(rows) and rows[n - 4].last:
                add("branch_hi", r=rows[n - 4])
            if 0 <= n - 5 < len(rows) and rows[n - 5].last:
                add("branch_lo", r=rows[n - 5])

    xsq_of = {}
    for layer in range(DEPTH):
        fill, pend = [], []
        def spread(n):
            for _ in range(min(n, len(fill))):
                fill.pop(0)()

        def normed_head(kind, c, g, width, then=None):
            def squares(turn_):
                s = square(kind, c, g, width)
                norms.append(lambda: norm(s, kind, c, kind, width, kind in ("fq", "fk")))
                if then is not None:
                    thens.append(then)
            return squares

        def step_group(n, make):
            make()
            for z in [z for z in pend if z[0] <= n and z[2] != "sq"]:
                pend.remove(z)
                z[1](n)
            while norms:
                done = norms.pop(0)()
                if thens:
                    f = thens.pop(0)
                    if f is not None:
                        pend.append((n + 1, f(done), "turn"))
            for z in [z for z in pend if z[0] <= n + 1 and z[2] == "sq"][:1]:
                pend.remove(z)
                z[1](n + 1)

        norms, thens = [], []
        if layer == 0:
            for t in range(NT):
                turn("x", t=t)
            turn("vectors")
            for c in range(KC):
                if c in (0, KC // 2):
                    add("first_panel", p=c // (KC // 2))
                add("split_x0", c=c, xs=take("xs"))
            for c in range(KC):
                square("x0", c, None, T)
            xsq_of[0] = count["sq"]
        add("load_mem", layer=layer, p=count["panel"])

        def mem_split(c):
            return lambda: add("mem_split", layer=layer, c=c, s=take("msq"), jobs=marks["memt", layer])

        now = 0
        order = [c for k in range(HC) for c in ((HC - 1 - k, HC + k) if layer == 0 else (HC + k, k))]
        for n, c in enumerate(order):
            kind = "q" if c >= HC else ("u" if layer == 0 else "fq")

            def make(n=n, c=c, kind=kind):
                g = group(colsof(w_in[layer], c * P, (c + 1) * P), P, "x", kind, c=c % HC,
                          first=n == 0, xs=layer * 2 * KC, layer=layer)
                if n == 0:
                    rjob[0] = take("job")
                    steps.insert(len(steps) - 1, Step(kind="r", m=rjob[0], r=take("r"), s=xsq_of[layer], layer=layer))
                    marks["r"] = steps[-2] if layer == 0 else None
                if n == 1:
                    steps[-2].r = marks["r"]
                if kind == "u":
                    def windows(turn_):
                        pn = take("pool")
                        add("windows", c=c, n=pn, g=count["acc"], o=take("win", c + 4))

                        def product_(turn_):
                            add("pool", c=c, m=take("job"), y=take("ys"), n=pn)
                        pend.append((turn_ + 1, product_, "pool"))
                    pend.append((n + 1, windows, "win"))
                else:
                    pend.append((n + 2, normed_head(kind, c % HC, g, T, None), "sq"))
            step_group(now, make)
            now += 1
            if n == 1 and layer == 0:
                marks["hist"] = turn("hist")
            if n == 1:
                for t in range(MK):
                    turn("mem", t=t, layer=layer)
                marks["memt", layer] = count["job"]
                fill += [mem_split(c_) for c_ in range(KC)]
                fill.append(lambda: add("load_caches", layer=layer, m=marks["memt", layer], mh=(layer + 1) * KC))
                fill.append(lambda: add("rm", m=take("job"), r=take("rm")))
                if layer == 1:
                    fill += [lambda c_=c_: add("split_kv", c=c_, ys=take("ys")) for c_ in range(KC)]
            if n >= 1:
                spread(2 if layer == 0 else 3)
        for c in [c_ for k in range(HC) for c_ in (k, HC + k)]:
            kind = "mk" if c < HC else "mv"

            def make(c=c, kind=kind):
                g = group(colsof(w_mem[layer], c * P, (c + 1) * P), P, "m", kind, c=c % HC,
                          first=c == 0, xs=layer * KC, layer=layer)
                if kind == "mk":
                    pend.append((now + 1, normed_head("mk", c, g, MT_TOK,
                                                      lambda n_: lambda turn_: turn("mk", c=c, n=n_, layer=layer)), "sq"))
                else:
                    pend.append((now + 1, lambda turn_: turn("mv", c=c % HC, g=g, layer=layer), "turn"))
            step_group(now, make)
            now += 1
            spread(1)
        if layer == 0:
            assert not fill
            turn("state")
            store("state", m=count["job"])
            turn("cmk", layer=layer)
            while pend:
                step_group(now, lambda: None)
                now += 1
            store("mem", layer=layer, m=count["job"])
        else:
            for c in [2 * HC] + [c_ for k in range(HC) for c_ in (k, HC + k)]:
                kind = "fk" if c < HC else ("fv" if c < 2 * HC else "gate")
                ncol = P if c < 2 * HC else FH

                def make(c=c, kind=kind, ncol=ncol):
                    spread(len(fill))
                    g = group(colsof(w_kv, c * P, c * P + ncol), ncol, "y", kind, c=c % HC,
                              first=kind == "gate", xs=0, layer=layer)

                    def stored(n_):
                        def turned(turn_):
                            m = turn("fk", c=c, n=n_)
                            store("fk", c=c, m=m)
                        return turned
                    if kind == "fk":
                        pend.append((now + 1, normed_head("fk", c, g, T, stored), "sq"))
                    elif kind == "fv":
                        pend.append((now + 1, lambda turn_: turn("fv", c=c % HC, g=g), "turn"))
                    else:
                        def gates(turn_):
                            turn("gate", g=g)
                            add("log_sigmoid", m=count["job"])
                            store("logf")
                            turn("cfk")
                            turn("cmk", layer=layer)
                            pend.append((turn_ + 2, lambda t_: add("cumsum", m=take("job")), "cumsum"))
                        pend.append((now + 1, gates, "turn"))
                step_group(now, make)
                now += 1
                if c == HC:
                    store("mem", layer=layer, m=count["job"])
            while pend:
                step_group(now, lambda: None)
                now += 1
            store("fv", m=count["job"])
        attend(layer, [("mem", range(HC))] if layer == 0 else [("mem", range(HC)), ("fox", range(FH))])
        p = count["panel"]
        for n in range(KC):
            panel(None, KC)
        if layer == 0:
            assert count["ys"] == KC
        resid(layer, "out", 1, p)
        p = count["panel"]
        for n in range(2 * FC):
            panel(None, KC)
        add("up", layer=layer, p=p, g=take("acc", 2 * FC), j=take("h", FC), xs=layer * 2 * KC + KC,
            m=take("job"), r=take("r"), s=count["sq"])
        rjob[0] = count["job"] - 1
        p = count["panel"]
        for n in range(KC):
            for s in range(4):
                panel(None, SUB[s])
        resid(layer, "down", 4, p)
        xsq_of[layer + 1] = count["sq"]
    NPANEL = count["panel"]
    GATE_STEPS = 8
    F_STEPS = 7
    DVE_CONSTS = 6 + sum(w - 1 for w in WINDOWS)

    base = 16640
    ctx = ExitStack()
    with ctx:
        def place(name, shape, dt, offset):
            return nc.alloc_sbuf_tensor_at(name, shape, dt, offset=offset)

        XB = KC * T * 4
        o_x = base
        o_xh = o_x + XB
        o_hh = o_xh + 2 * XB
        o_hl = o_hh + FC * T * 4
        o_raw = o_hl + FC * T * 4
        o_wh = o_raw + RAW_SLOTS * KC * P * 4
        o_wl = o_wh + SPLIT_SLOTS * KC * P * 4
        o_e = o_wl + SPLIT_SLOTS * KC * P * 4
        X = place("X", [P, KC, T], F32, o_x)
        XH = place("XH", [P, KC, T], F32R, o_xh)
        XL = place("XL", [P, KC, T], F32R, o_xh + XB)
        HH = place("HH", [P, FC, T], F32R, o_hh)
        HL = place("HL", [P, FC, T], F32R, o_hl)
        RAW = place("RAW", [P, RAW_SLOTS, KC, P], F32, o_raw)
        WH = place("WH", [P, SPLIT_SLOTS, KC, P], F32R, o_wh)
        WL = place("WL", [P, SPLIT_SLOTS, KC, P], F32R, o_wl)

        top = [o_e]

        def small(name, shape, dt):
            size = 2 if dt == BF16 else 4
            for n in shape[1:]:
                size *= n
            size = (size + 31) // 32 * 32
            t = place(name, shape, dt, top[0])
            top[0] += size
            assert top[0] <= 229344, name
            return t

        R = small("R", [P, T], F32)
        RM = small("RM", [P, MT_TOK], F32)
        SQ = small("SQ", [P, 2, T], F32)
        ACC = small("ACC", [P, T], F32)
        TG = small("TG", [P, T], F32)
        TU = small("TU", [P, T], F32)
        TGU = [TG, TU]
        MSQ = [slice(0, MT_TOK), slice(MT_TOK, 2 * MT_TOK)]
        IDENT = small("IDENT", [P, P], F32)
        ONES = small("ONES", [P, P], F32)
        BLK = small("BLK", [P, P], F32)
        IDB = small("IDB", [P, P], BF16)
        MASK = small("MASK", [P, P], BF16)
        NVEC = 8 * 7 + 4 + HC + 2
        VROW = small("VROW", [NVEC, P], F32)
        VEC = small("VEC", [P, NVEC], F32)
        GQ = small("GQ", [P, 4], F32)
        BF = small("BF", [FH, 1], F32)
        EPSC = small("EPSC", [P, 2], F32)
        INVC = small("INVC", [P, HC, 16], F32)
        STAT = small("STAT", [P, 3, 4], F32)
        FP = small("FP", [96, L + PAST + LS], BF16)
        NFP = small("NFP", [96, L + PAST + LS], BF16)
        CL = small("CL", [P, PK, FH], F32)
        G_MIX, G_FFN, G_KV, G_MEM = 0, 16, 32, 40
        QN_M, KN_M, PSC, QN_F, KN_F = 56, 58, 60, 64, 65

        a0 = o_hh + XB
        b0 = o_hl + XB
        c0 = o_xh
        MB = KC * MT_TOK * 4
        MH = place("MH", [P, KC, MT_TOK], F32R, a0)
        ML = place("ML", [P, KC, MT_TOK], F32R, b0)
        MTR = place("MTR", [P, KC, MT_TOK], F32, a0 + MB)
        MRAW = place("MRAW", [P, MK, D], F32, b0 + MB)
        UW = HIST + L + HIST + LS
        U = place("U", [P, HC, UW], F32, a0 + 2 * MB)
        FQ = place("FQ", [P, HC, T], F32, a0 + 2 * MB)
        o_l3 = a0 + 2 * MB + HC * UW * 4
        L3 = place("L3", [P, NT + PK, 96], F32, o_l3)
        WP = place("WP", [P, HC, P], F32, o_l3)
        TRI = place("TRI", [P, L], F32, o_l3 + (NT + PK) * 96 * 4)
        assert o_l3 + (NT + PK) * 96 * 4 + L * 4 <= o_hl
        ZQ = place("ZQ", [P, HC, T], F32, b0 + 2 * MB)
        o_cfv = b0 + 2 * MB + HC * T * 4
        CFV = place("CFV", [P, PK, W2], F32, o_cfv)
        HRAW = place("HRAW", [HIST, W2], F32, o_cfv)
        SEL = place("SEL", [96, FH, P], BF16, o_cfv + PK * W2 * 4)
        assert o_cfv + PK * W2 * 4 + FH * P * 2 <= o_raw
        PR = place("PR", [P, 3, 512], F32, a0)
        FT = place("FT", [96, L + PAST + LS], F32, a0)
        PT = place("PT", [P, 2, 512], F32, b0)
        STG = [place("STG0", [P, NT, P], F32, b0 + MB + 4096), place("STG1", [P, NT, P], F32, b0 + 4096)]
        CMK = place("CMK", [P, MK, W2], F32, a0 + MB)
        CFK = place("CFK", [P, PK, W2], F32, a0 + MB + 4096)
        PST = place("PST", [HIST, 2, W2], F32, a0 + MB + 4096)
        CMV = place("CMV", [P, MK, W2], F32, b0 + MB)
        XR = place("XR", [P, TT, D], F32, o_hh)
        XRS = place("XRS", [LS, D], F32, o_hl)
        FK = place("FK", [P, HC, T], F32, c0)
        PW = place("PW", [P, 2, UW], F32, o_hl + XB // 2)
        o_vt = c0 + HC * T * 4
        VT = place("VT", [P, NT, W2], F32, o_vt)
        MKTOK = place("MKTOK", [P, MK, W2], F32, o_vt)
        PD = place("PD", [P, 2, T], F32, o_hh + XB // 2)
        o_c1 = o_vt + NT * W2 * 4
        CFKT = place("CFKT", [P, HC, PAST], F32, o_c1)
        MKT = place("MKT", [P, HC, MT_TOK], F32, o_c1 + 4096)
        MV = place("MV", [P, MK, W2], F32, o_c1 + 8192)
        CMKT = place("CMKT", [P, HC, MT_TOK], F32, o_c1 + 12288)
        YST = [place(f"YST{k}", [P, NT, P], F32, c0 + k * NT * P * 4) for k in range(2)]
        assert o_c1 + 16384 <= o_hh
        LG = small("LG", [P, 6, NT, FH], F32)

        ACCP = ctx.enter_context(nc.psum_tensor("ACCP", [P, 2, 2, 512], F32))
        MISC = ctx.enter_context(nc.psum_tensor("MISC", [P, 2, 2, 512], F32))

        def sem(name):
            return ctx.enter_context(nc.semaphore(name))

        raw_loaded = [sem(f"raw_loaded{i}") for i in range(RAW_SLOTS)]
        hi_ready, lo_ready = sem("hi_ready"), sem("lo_ready")
        panel_used, acc_free = sem("panel_used"), sem("acc_free")
        misc_done, misc_free = sem("misc_done"), sem("misc_free")
        sq_ready, sq_free = sem("sq_ready"), sem("sq_free")
        msq_ready, msq_free = sem("msq_ready"), sem("msq_free")
        half_taken = sem("half_taken")
        xh_ready, xl_ready = sem("xh_ready"), sem("xl_ready")
        yh_ready, yl_ready = sem("yh_ready"), sem("yl_ready")
        mh_ready, ml_ready = sem("mh_ready"), sem("ml_ready")
        r_ready, rm_ready = sem("r_ready"), sem("rm_ready")
        ln_done = sem("ln_done")
        inv_ready = sem("inv_ready")
        silu_done, h_ready = sem("silu_done"), sem("h_ready")
        hh_ready, hl_ready = sem("hh_ready"), sem("hl_ready")
        scores_ready, max_ready, probs_ready = sem("scores_ready"), sem("max_ready"), sem("probs_ready")
        recip_ready, probs_normed = sem("recip_ready"), sem("probs_normed")
        probs_turned, pt_ready, pv_done = sem("probs_turned"), sem("pt_ready"), sem("pv_done")
        vec_loaded, mem_loaded, xin_loaded = sem("vec_loaded"), sem("mem_loaded"), [sem(f"xin{t}") for t in range(NT)]
        caches_loaded, hist_loaded, wp_loaded = sem("caches_loaded"), sem("hist_loaded"), sem("wp_loaded")
        fox_loaded, clf_loaded = sem("fox_loaded"), sem("clf_loaded")
        mem_stored, misc_stored = sem("mem_stored"), sem("misc_stored")
        fk_stored = [sem(f"fk_stored{k}") for k in range(2)]
        y_stored = [sem(f"y_stored{k}") for k in range(2)]
        y_last_stored = sem("y_last_stored")
        consts, consts_dve = sem("consts"), sem("consts_dve")
        acc_zeroed = sem("acc_zeroed")
        window_done, pooled_in, yl_pooled = sem("window_done"), sem("pooled_in"), sem("yl_pooled")
        pads_ready = sem("pads_ready")
        gate_steps, gate_act = sem("gate_steps"), sem("gate_act")
        f_steps = sem("f_steps")
        sel_ready = sem("sel_ready")
        f_evac = sem("f_evac")

        block = ctx.enter_context(nc.Block())

        def halves(w):
            return [(0, w)] if w <= 512 and w != T else [(0, HALF), (HALF, T)]

        def moving_of(kind):
            return {"x": (XH, XL, xl_ready, T), "y": (HH, HL, yl_ready, T),
                    "m": (MH, ML, ml_ready, MT_TOK)}[kind]

        BUF = {"q": ZQ, "fq": FQ, "mk": MKT, "fk": FK}

        def r_scale(act, a, m, r):
            for k, (lo, hi) in enumerate(halves(T)):
                a.activation(R[:, lo:hi], MISC[:, m % 2, k, 0:hi - lo], ACT.Ln, bias=EPSC[:, 0:1], scale=1.0 / D)\
                    .then_inc(misc_free if k else ln_done, 1)
            act.wait_ge(misc_free, m + 1)
            a.activation(R[:], R[:], ACT.Exp, scale=-0.5).then_inc(r_ready, 1)

        def evac(s, dve, v):
            dve.wait_ge(panel_used, s.p + 1)
            ps = ACCP[:, s.g % 2]
            if s.evac in ("mk", "mv"):
                dve.wait_ge(rm_ready, s.layer + 1)
                dst = MKT[:, s.c] if s.evac == "mk" else TGU[s.c % 2][:, 0:MT_TOK]
                v.tensor_tensor(dst, ps[:, 0, 0:MT_TOK], RM[:], ALU.mult).then_inc(acc_free, 1)
                return
            dve.wait_ge(r_ready, 2 * s.layer + 1)
            if s.evac == "u":
                for dst, b, lo, hi, r0 in ((HIST, 0, 0, HALF, 0), (HIST + HALF, 1, 0, L - HALF, HALF),
                                           (2 * HIST + L, 1, L - HALF, HALF, L)):
                    v.tensor_tensor(U[:, s.c, dst:dst + hi - lo], ps[:, b, lo:hi], R[:, r0:r0 + hi - lo], ALU.mult)\
                        .then_inc(acc_free if r0 == L else half_taken, 1)
                return
            if s.evac == "gate":
                for b, (lo, hi) in enumerate(halves(T)):
                    v.tensor_tensor(TG[0:FH, lo:hi], ps[0:FH, b, 0:hi - lo], R[0:FH, lo:hi], ALU.mult).then_inc(f_evac, 1)
                dve.wait_ge(f_evac, 2)
                dve.wait_ge(clf_loaded, 32)
                v.tensor_scalar(TG[0:FH], TG[0:FH], BF[:, 0:1], None, ALU.add).then_inc(acc_free, 1)
                return
            dst = {"q": ZQ[:, s.c], "fq": FQ[:, s.c], "fk": FK[:, s.c], "fv": TGU[s.c % 2][:]}[s.evac]
            for b, (lo, hi) in enumerate(halves(T)):
                v.tensor_tensor(dst[:, lo:hi], ps[:, b, 0:hi - lo], R[:, lo:hi], ALU.mult)\
                    .then_inc(acc_free if b else half_taken, 1)

        def windows(s, dve, v):
            w = WINDOWS[s.c]
            done = s.o
            dve.wait_ge(acc_free, s.g)
            dve.wait_ge(misc_free, marks["hist"] + 1)
            dve.wait_ge(pads_ready, 1)
            dve.wait_ge(consts_dve, DVE_CONSTS)
            sums = U[:, s.c]
            for n in range(s.c + 1):
                lo = 2 ** (n + 1) - 1
                if done:
                    dve.wait_ge(window_done, done)
                v.tensor_tensor(PW[:, n % 2, lo:UW], sums[:, lo:UW], sums[:, lo - 2 ** n:UW - 2 ** n], ALU.add).then_inc(window_done, 1)
                done += 1
                sums = PW[:, n % 2]
            if s.n >= 2:
                dve.wait_ge(yl_pooled, s.n - 1)
            dve.wait_ge(window_done, done)
            d, u = PD[:, s.n % 2], U[:, s.c]
            q0, s0 = HIST, 2 * HIST + L
            v.scalar_tensor_tensor(d[:, w - 1:L], sums[:, q0 + w - 1:q0 + L], 1.0 / w, u[:, q0 + w - 1:q0 + L], ALU.mult, ALU.subtract).then_inc(window_done, 1)
            v.scalar_tensor_tensor(d[:, L:T], sums[:, s0:s0 + LS], 1.0 / w, u[:, s0:s0 + LS], ALU.mult, ALU.subtract).then_inc(window_done, 1)
            v.tensor_tensor(d[:, 0:w - 1], sums[:, q0:q0 + w - 1], INVC[:, s.c, 0:w - 1], ALU.mult).then_inc(window_done, 1)
            dve.wait_ge(window_done, done + 3)
            v.tensor_tensor(d[:, 0:w - 1], d[:, 0:w - 1], u[:, q0:q0 + w - 1], ALU.subtract).then_inc(pooled_in, 1)

        def pool(s, dve, v):
            dve.wait_ge(yh_ready, s.y + 1)
            dve.wait_ge(misc_free, s.m + 1)
            v.tensor_tensor(HL[:, s.c], PD[:, s.n % 2], HH[:, s.c], ALU.subtract).then_inc(yl_pooled, 1)

        def scale_probs(r, dve, v):
            dve.wait_ge(probs_ready, r.u + 1)
            v.reciprocal(STAT[0:r.nq, 2, r.u % 4:r.u % 4 + 1], STAT[0:r.nq, 1, r.u % 4:r.u % 4 + 1]).then_inc(recip_ready, 1)
            dve.wait_ge(recip_ready, r.u + 1)
            pr = PR[0:r.nq, r.u % 3, 0:r.nk]
            v.tensor_scalar(pr, pr, STAT[0:r.nq, 2, r.u % 4:r.u % 4 + 1], None, ALU.mult).then_inc(probs_normed, 1)

        VECTORS = [(G_MIX, G_MIX + 16, ins["g_mix"].rearrange("l (k p) -> (l k) p", p=P)),
                   (G_FFN, G_FFN + 16, ins["g_ffn"].rearrange("l (k p) -> (l k) p", p=P)),
                   (G_KV, G_KV + 8, ins["g_kv"].rearrange("(k p) -> k p", p=P)),
                   (G_MEM, G_MEM + 16, ins["g_mem"].rearrange("l (k p) -> (l k) p", p=P)),
                   (QN_M, QN_M + 2, ins["q_norm_mem"]), (KN_M, KN_M + 2, ins["k_norm_mem"]),
                   (PSC, PSC + HC, ins["pool_scale"].rearrange("l (k p) -> (l k) p", p=P))]

        @block.sync
        def _(sp):
            def load(p, src, per=0, i=0):
                nk, ncol = panel_shape[p]
                src = src if not callable(src) else src()
                if p >= RAW_SLOTS:
                    sp.wait_ge(lo_ready, at(p - RAW_SLOTS + 1, per, i))
                sp.dma_start(RAW[:, p % RAW_SLOTS, 0:nk, 0:ncol], src).then_inc(raw_loaded[p % RAW_SLOTS], 16)

            for tt in range(TT):
                sp.dma_start(XR[:, tt], x_prompt[0, tt * P:(tt + 1) * P]).then_inc(xin_loaded[tt], 16)
                if tt == 0:
                    sp.dma_start(XRS[:], x_sample[0]).then_inc(xin_loaded[TT], 16)
            for n0, n1, src in VECTORS[4:]:
                sp.dma_start(VROW[n0:n1], src).then_inc(vec_loaded, 16)
            for e in range(2):
                sp.dma_start(VROW[QN_F:QN_F + 1, e * FD:(e + 1) * FD], ins["q_norm_fox"]).then_inc(vec_loaded, 16)
                sp.dma_start(VROW[KN_F:KN_F + 1, e * FD:(e + 1) * FD], ins["k_norm_fox"].rearrange("(a d) -> a d", a=1)).then_inc(vec_loaded, 16)
            load(0, next(s for s in steps if s.p == 0 and s.kind == "group").view)
            sp.wait_ge(xin_loaded[TT - 1], 16)
            for s in steps:
                if s.kind == "group":
                    if s.p:
                        load(s.p, s.view)
                elif s.kind == "resid" and s.which == "out":
                    with sp.Fori(0, KC // 4) as i:
                        cols = [sp.snap(i * (4 * P) + k * P) for k in range(4)]
                        for k in range(4):
                            load(s.p + k, w_out[s.layer][:, :, bass.ds(cols[k], P)], 4, i)
                elif s.kind == "resid":
                    with sp.Fori(0, KC) as i:
                        col = sp.snap(i * P)
                        for k in range(4):
                            load(s.p + k, w_down[s.layer][:, SUB0[k]:SUB0[k] + SUB[k], bass.ds(col, P)], 4, i)
                    if s.final:
                        sp.wait_ge(misc_free, s.m + KC)
                        sp.dma_start(outs["y_prompt"][0].rearrange("(t p) d -> p t d", p=P)[:, :, D - P:D],
                                     YST[1][:, 0:TT]).then_inc(y_last_stored, 16)
                elif s.kind == "up":
                    with sp.Fori(0, FC // 2) as i:
                        cols = [sp.snap(i * (2 * P) + (k // 2) * P + (k % 2) * FF) for k in range(4)]
                        for k in range(4):
                            load(s.p + k, w_gu[s.layer][:, :, bass.ds(cols[k], P)], 4, i)

        @block.gpsimd
        def _(gp):
            g = nc.gpsimd
            g.memset(IDENT[:], 0.0).then_inc(consts, 1)
            g.memset(IDB[:], 0.0).then_inc(consts, 1)
            g.memset(MASK[:], 0.0).then_inc(consts, 1)
            gp.wait_ge(consts, 3)
            g.affine_select(out=IDENT[:], in_=IDENT[:], compare_op=ALU.not_equal, fill=1.0, base=0,
                            pattern=[[-1, P]], channel_multiplier=1).then_inc(consts, 1)
            g.affine_select(out=IDB[:], in_=IDB[:], compare_op=ALU.not_equal, fill=1.0, base=0,
                            pattern=[[-1, P]], channel_multiplier=1).then_inc(consts, 1)
            g.affine_select(out=MASK[:], in_=MASK[:], compare_op=ALU.is_ge, fill=NEG, base=0,
                            pattern=[[-1, P]], channel_multiplier=1).then_inc(consts, 1)
            gp.dma_start(BF[:], ins["b_f"].rearrange("(h a) -> h a", a=1)).then_inc(clf_loaded, 16)
            gp.dma_start(CL[:], ins["cache_fox_logf"][0].rearrange("(t p) h -> p t h", p=P)).then_inc(clf_loaded, 16)
            gp.dma_start(WP[:], ins["w_pool"][0].rearrange("g c d -> c g d")).then_inc(wp_loaded, 16)
            gp.dma_start(HRAW[:], ins["state_pool"][0, 0]).then_inc(hist_loaded, 16)

            def out(dst, src, stored):
                gp.dma_start(dst, src).then_inc(stored, 16)

            for s in steps:
                if s.kind == "load_mem":
                    if s.p:
                        gp.wait_ge(panel_used, s.p)
                    else:
                        gp.wait_ge(xin_loaded[TT - 1], 16)
                    gp.dma_start(MRAW[:], ins["mem_prompt"][0].rearrange("(t p) d -> p t d", p=P)).then_inc(mem_loaded, 16)
                    if s.layer == 1:
                        gp.wait_ge(misc_done, marks["hist"] + 1)
                        gp.dma_start(CFV[:], ins["cache_fox_v"][0].rearrange("(t p) h d -> p t (h d)", p=P)).then_inc(fox_loaded, 16)
                        g.memset(SEL[:], 0.0).then_inc(sel_ready, 1)
                        g.memset(TRI[:], 1.0).then_inc(sel_ready, 1)
                        gp.wait_ge(sel_ready, 2)
                        g.affine_select(out=TRI[:], in_=TRI[:], compare_op=ALU.is_ge, fill=0.0, base=0,
                                        pattern=[[1, L]], channel_multiplier=-1).then_inc(sel_ready, 1)
                        for j in range(3):
                            g.affine_select(out=SEL[:], in_=SEL[:], compare_op=ALU.not_equal, fill=1.0, base=-32 * j,
                                            pattern=[[-1, FH], [0, P]], channel_multiplier=1).then_inc(sel_ready, 1)
                            gp.wait_ge(sel_ready, 4 + j)
                elif s.kind == "load_caches":
                    gp.wait_ge(ml_ready, s.mh)
                    gp.wait_ge(misc_done, s.m)
                    gp.dma_start(CMK[:], ins["cache_mem_k"][s.layer, 0].rearrange("(t p) h d -> p t (h d)", p=P)).then_inc(caches_loaded, 16)
                    gp.dma_start(CMV[:], ins["cache_mem_v"][s.layer, 0].rearrange("(t p) h d -> p t (h d)", p=P)).then_inc(caches_loaded, 16)
                    if s.layer == 1:
                        gp.dma_start(CFK[:], ins["cache_fox_k"][0].rearrange("(t p) h d -> p t (h d)", p=P)).then_inc(fox_loaded, 16)
                elif s.kind == "store" and s.name == "mem":
                    gp.wait_ge(misc_free, s.m)
                    out(outs["mem_k_prompt"][s.layer, 0].rearrange("(t p) h d -> p t (h d)", p=P), MKTOK[:], mem_stored)
                    out(outs["mem_v_prompt"][s.layer, 0].rearrange("(t p) h d -> p t (h d)", p=P), MV[:], mem_stored)
                elif s.kind == "store" and s.name == "state":
                    gp.wait_ge(misc_free, s.m)
                    out(outs["pool_state_prompt"][0, 0], PST[:, 0], misc_stored)
                    out(outs["pool_state_sample"][0, 0], PST[:, 1], misc_stored)
                elif s.kind == "store" and s.name == "fk":
                    gp.wait_ge(misc_free, s.m + 1)
                    st = STG[s.c % 2]
                    out(outs["fox_k_prompt"][0].rearrange("(t p) h d -> p t (h d)", p=P)[:, :, s.c * P:(s.c + 1) * P], st[:, 0:TT], fk_stored[s.c % 2])
                    out(outs["fox_k_sample"][0].rearrange("t h d -> t (h d)")[:, s.c * P:(s.c + 1) * P], st[0:LS, TT], fk_stored[s.c % 2])
                elif s.kind == "store" and s.name == "fv":
                    gp.wait_ge(misc_free, s.m)
                    out(outs["fox_v_prompt"][0].rearrange("(t p) h d -> p t (h d)", p=P), VT[:, 0:TT], misc_stored)
                    out(outs["fox_v_sample"][0].rearrange("t h d -> t (h d)"), VT[0:LS, TT], misc_stored)
                elif s.kind == "store" and s.name == "logf":
                    gp.wait_ge(gate_steps, GATE_STEPS)
                    out(outs["fox_logf_prompt"][0].rearrange("(t p) h -> p t h", p=P), LG[:, 0, 0:TT], misc_stored)
                    out(outs["fox_logf_sample"][0], LG[0:LS, 0, TT], misc_stored)
                elif s.kind == "resid" and s.layer == DEPTH - 1 and s.which == "down":
                    yp = outs["y_prompt"][0].rearrange("(t p) d -> p t d", p=P)
                    with gp.Fori(0, KC // 2 - 1) as i:
                        for k in range(2):
                            col = gp.snap(i * (2 * P) + k * P)
                            gp.wait_ge(misc_free, at(s.m + k + 1, 2, i))
                            gp.dma_start(yp[:, :, bass.ds(col, P)], YST[k][:, 0:TT]).then_inc(y_stored[k], 16)
                            gp.dma_start(outs["y_sample"][0][:, bass.ds(col, P)], YST[k][0:LS, TT]).then_inc(y_stored[k], 16)
                    gp.wait_ge(misc_free, s.m + KC - 1)
                    gp.dma_start(yp[:, :, D - 2 * P:D - P], YST[0][:, 0:TT]).then_inc(y_stored[0], 16)
                    gp.dma_start(outs["y_sample"][0][:, D - 2 * P:D - P], YST[0][0:LS, TT]).then_inc(y_stored[0], 16)
            gp.wait_ge(mem_stored, 32 * DEPTH)
            gp.wait_ge(misc_stored, 96)
            for k in range(2):
                gp.wait_ge(fk_stored[k], 16 * HC)
                gp.wait_ge(y_stored[k], 16 * KC - 32 * k)
            gp.wait_ge(y_last_stored, 32)

        @block.scalar
        def _(act):
            a = nc.scalar
            for n0, n1, src in VECTORS[:4]:
                act.dma_start(VROW[n0:n1], src).then_inc(vec_loaded, 16)

            def split_hi(q, per=0, i=0):
                if q >= NPANEL:
                    return
                nk, ncol = panel_shape[q]
                act.wait_ge(raw_loaded[q % RAW_SLOTS], at(16 * (q // RAW_SLOTS + 1), 4 * per, i))
                if q >= SPLIT_SLOTS:
                    act.wait_ge(panel_used, at(q - SPLIT_SLOTS + 1, per, i))
                a.activation(WH[:, q % SPLIT_SLOTS, 0:nk, 0:ncol], RAW[:, q % RAW_SLOTS, 0:nk, 0:ncol],
                             ACT.Copy).then_inc(hi_ready, 1)

            a.preload_act_table_set("natural_log_exp_and_others")
            for s in steps:
                if s.kind == "first_panel":
                    split_hi(s.p)
                elif s.kind == "group":
                    split_hi(s.p + 2)
                elif s.kind == "turn":
                    act.wait_ge(misc_done, s.m + 1)
                    ps = MISC[:, s.m % 2]
                    if s.name == "vectors":
                        a.activation(VEC[:], ps[:, 0, 0:NVEC], ACT.Copy).then_inc(misc_free, 1)
                        act.wait_ge(misc_free, s.m + 1)
                        a.activation(GQ[:, 0:2], VEC[:, QN_M:QN_M + 2], ACT.Copy, scale=float(P) ** -0.5).then_inc(gate_act, 1)
                        a.activation(GQ[:, 2:3], VEC[:, QN_F:QN_F + 1], ACT.Copy, scale=float(FD) ** -0.5).then_inc(gate_act, 1)
                    elif s.name == "x":
                        n = P if s.t < TT else LS
                        src = ps[:, :, :].rearrange("p b (k t) -> p (b k) t", t=P)[:, :, 0:n]
                        a.activation(X[:, :, s.t * P:s.t * P + n], src, ACT.Copy).then_inc(misc_free, 1)
                    elif s.name == "mem":
                        src = ps[:, :, :].rearrange("p b (k t) -> p (b k) t", t=P)
                        a.activation(MTR[:, :, s.t * P:(s.t + 1) * P], src, ACT.Copy).then_inc(misc_free, 1)
                    elif s.name == "hist":
                        src = ps[:, 0, 0:HC * 16].rearrange("p (k t) -> p k t", t=16)[:, :, 0:HIST]
                        a.activation(U[:, :, HIST + L:2 * HIST + L], src, ACT.Copy).then_inc(misc_free, 1)
                    elif s.name == "mk":
                        a.activation(MKTOK[:, :, s.c * P:(s.c + 1) * P],
                                     ps[:, 0, 0:MT_TOK].rearrange("p (t c) -> p t c", c=P), ACT.Copy).then_inc(misc_free, 1)
                    elif s.name == "mv":
                        a.activation(MV[:, :, s.c * P:(s.c + 1) * P],
                                     ps[:, 0, 0:MT_TOK].rearrange("p (t c) -> p t c", c=P), ACT.Copy).then_inc(misc_free, 1)
                    elif s.name in ("cmk", "cfk"):
                        dst = CMKT if s.name == "cmk" else CFKT
                        a.activation(dst[:], ps.rearrange("p b (k t) -> p (b k) t", t=2 * P), ACT.Copy).then_inc(misc_free, 1)
                    elif s.name == "state":
                        a.activation(PST[:], ps[0:HIST], ACT.Copy).then_inc(misc_free, 1)
                    elif s.name == "fk":
                        if s.c >= 2:
                            act.wait_ge(fk_stored[s.c % 2], 32)
                        st = STG[s.c % 2]
                        a.activation(st[:, 0:TT], ps[:, 0].rearrange("p (t c) -> p t c", c=P), ACT.Copy).then_inc(ln_done, 1)
                        a.activation(st[0:LS, TT], ps[0:LS, 1, 0:P], ACT.Copy).then_inc(misc_free, 1)
                    elif s.name == "fv":
                        if s.c == 0:
                            act.wait_ge(mem_stored, 32 * DEPTH)
                        a.activation(VT[:, 0:TT, s.c * P:(s.c + 1) * P], ps[:, 0].rearrange("p (t c) -> p t c", c=P), ACT.Copy).then_inc(ln_done, 1)
                        a.activation(VT[0:LS, TT, s.c * P:(s.c + 1) * P], ps[0:LS, 1, 0:P], ACT.Copy).then_inc(misc_free, 1)
                    elif s.name == "gate":
                        act.wait_ge(consts_dve, DVE_CONSTS)
                        a.activation(LG[:, 1, 0:TT], ps[:, 0, 0:TT * FH].rearrange("p (t h) -> p t h", h=FH), ACT.Copy).then_inc(ln_done, 1)
                        a.activation(LG[0:LS, 1, TT], ps[0:LS, 0, TT * FH:NT * FH], ACT.Copy).then_inc(misc_free, 1)
                elif s.kind == "square":
                    if s.g is not None:
                        act.wait_ge(acc_free, s.g + 1)
                        src = BUF[s.buf][:, s.c]
                    else:
                        act.wait_ge(misc_free, NT + 1)
                        src = X[:, s.c]
                    if s.s >= 2:
                        act.wait_ge(sq_free, s.s - 1)
                    a.activation(SQ[:, s.s % 2, 0:s.width], src, ACT.Square).then_inc(sq_ready, 1)
                elif s.kind == "split_x0":
                    act.wait_ge(misc_free, NT + 1)
                    a.activation(XH[:, s.c], X[:, s.c], ACT.Copy, scale=VEC[:, G_MIX + s.c:G_MIX + s.c + 1]).then_inc(xh_ready, 1)
                elif s.kind == "split_kv":
                    a.activation(HH[:, s.c], X[:, s.c], ACT.Copy, scale=VEC[:, G_KV + s.c:G_KV + s.c + 1]).then_inc(yh_ready, 1)
                elif s.kind == "mem_split":
                    act.wait_ge(misc_free, s.jobs)
                    if s.s >= 2:
                        act.wait_ge(msq_free, s.s - 1)
                    a.activation(TU[:, MSQ[s.s % 2]], MTR[:, s.c], ACT.Square).then_inc(msq_ready, 1)
                    v = G_MEM + KC * s.layer + s.c
                    a.activation(MH[:, s.c], MTR[:, s.c], ACT.Copy, scale=VEC[:, v:v + 1]).then_inc(mh_ready, 1)
                elif s.kind in ("r", "rm"):
                    act.wait_ge(misc_done, s.m + 1)
                    if s.kind == "r":
                        r_scale(act, a, s.m, s.r)
                    else:
                        a.activation(RM[:], MISC[:, s.m % 2, 0, 0:MT_TOK], ACT.Ln, bias=EPSC[:, 0:1], scale=1.0 / D).then_inc(misc_free, 1)
                        act.wait_ge(misc_free, s.m + 1)
                        a.activation(RM[:], RM[:], ACT.Exp, scale=-0.5).then_inc(rm_ready, 1)
                elif s.kind == "norm":
                    act.wait_ge(misc_done, s.m + 1)
                    n = FD if s.block else P
                    hv = halves(s.width)
                    for k, (lo, hi) in enumerate(hv):
                        a.activation(SQ[:, s.s % 2, lo:hi], MISC[:, s.m % 2, k, 0:hi - lo], ACT.Ln, bias=EPSC[:, 0:1], scale=1.0 / n)\
                            .then_inc(misc_free if k == len(hv) - 1 else ln_done, 1)
                    act.wait_ge(misc_free, s.m + 1)
                    a.activation(SQ[:, s.s % 2, 0:s.width], SQ[:, s.s % 2, 0:s.width], ACT.Exp, scale=-0.5).then_inc(inv_ready, 1)
                elif s.kind == "pool":
                    act.wait_ge(misc_done, s.m + 1)
                    scale = VEC[:, PSC + s.c:PSC + s.c + 1]
                    for k, (lo, hi) in enumerate(halves(T)):
                        a.activation(HH[:, s.c, lo:hi], MISC[:, s.m % 2, k, 0:hi - lo], ACT.Copy, scale=scale).then_inc(yh_ready if k else ln_done, 1)
                    for k, (lo, hi) in enumerate(halves(T)):
                        a.activation(PD[:, s.n % 2, lo:hi], MISC[:, s.m % 2, k, 0:hi - lo], ACT.Copy, scale=scale).then_inc(misc_free if k else ln_done, 1)
                elif s.kind == "log_sigmoid":
                    act.wait_ge(gate_steps, 1)
                    a.activation(LG[:, 3], LG[:, 2], ACT.Exp, scale=-1.0).then_inc(gate_act, 1)
                    act.wait_ge(gate_steps, 2)
                    a.activation(LG[:, 5], LG[:, 4], ACT.Ln).then_inc(gate_act, 1)
                elif s.kind == "cumsum":
                    act.wait_ge(misc_done, s.m + 1)
                    a.activation(FT[:, 0:L], MISC[0:96, s.m % 2, 0], ACT.Copy).then_inc(ln_done, 1)
                    a.activation(FT[:, L:], MISC[0:96, s.m % 2, 1, 0:PAST + LS], ACT.Copy).then_inc(misc_free, 1)
                elif s.kind == "exp":
                    r = s.r
                    act.wait_ge(max_ready, r.u + 1)
                    if r.u >= 3:
                        act.wait_ge(probs_turned, r.u - 2)
                    if r.first and r.layer == 1:
                        act.wait_ge(f_steps, F_STEPS)
                    a.activation(PR[0:r.nq, r.u % 3, 0:r.nk], MISC[0:r.nq, 0, r.u % 2, 0:r.nk], ACT.Exp,
                                 bias=STAT[0:r.nq, 0, r.u % 4:r.u % 4 + 1],
                                 accum_out=STAT[0:r.nq, 1, r.u % 4:r.u % 4 + 1]).then_inc(probs_ready, 1)
                elif s.kind == "turn_probs":
                    r = s.r
                    act.wait_ge(probs_turned, r.u + 1)
                    if r.u >= 2:
                        act.wait_ge(pv_done, r.u - 1)
                    ps = MISC[:, 1, r.u % 2].rearrange("p (k q) -> p k q", q=P)
                    pt = PT[:, r.u % 2].rearrange("p (k q) -> p k q", q=P)
                    full = r.nk // P
                    rest = r.nk % P
                    a.activation(pt[:, 0:full, 0:r.nq], ps[:, 0:full, 0:r.nq], ACT.Copy).then_inc(ln_done if rest else pt_ready, 1)
                    if rest:
                        a.activation(pt[0:rest, full, 0:r.nq], ps[0:rest, full, 0:r.nq], ACT.Copy).then_inc(pt_ready, 1)
                elif s.kind == "branch_hi":
                    r = s.r
                    act.wait_ge(pv_done, r.u + 1)
                    c = r.c + (HC if r.att == "mem" else 0)
                    a.activation(HH[:, c, 0:L], ACCP[:, r.g % 2, 0, 0:L], ACT.Copy).then_inc(ln_done, 1)
                    a.activation(HH[:, c, L:T], ACCP[:, r.g % 2, 1, 0:LS], ACT.Copy).then_inc(yh_ready, 1)
                elif s.kind == "resid":
                    gain = (G_FFN + KC * s.layer) if s.which == "out" else (G_MIX + KC)
                    if s.which == "out":
                        act.wait_ge(mem_stored, 32 * (s.layer + 1))
                        act.wait_ge(misc_stored, 32 if s.layer == 0 else 96)
                        if s.layer == 1:
                            act.wait_ge(fk_stored[0], 16 * HC)
                            act.wait_ge(fk_stored[1], 16 * HC)

                    def take_y(k, turn_, i, s=s):
                        act.wait_ge(misc_done, at(s.m + turn_ + 1, s.body, i))
                        if turn_ >= 0:
                            if not isinstance(i, int) or i or turn_ > 1:
                                act.wait_ge(y_stored[k], at(32 * (turn_ // 2), 32, i))
                        elif not isinstance(i, int) or i > 1:
                            act.wait_ge(y_stored[k], at(-32, 32, i))
                        ps = MISC[:, (s.m + turn_) % 2]
                        a.activation(YST[k][:, 0:TT], ps[:, 0].rearrange("p (t c) -> p t c", c=P), ACT.Copy).then_inc(ln_done, 1)
                        a.activation(YST[k][0:LS, TT], ps[0:LS, 1, 0:P], ACT.Copy).then_inc(misc_free, 1)

                    def body(i, last, s=s, gain=gain):
                        nb, ns = s.body, s.nsub
                        for k in range(nb):
                            for q in range(ns):
                                if last:
                                    split_hi(s.p + (nb * i + k) * ns + q + 2)
                                else:
                                    split_hi(s.p + k * ns + q + 2, nb * ns, i)
                            if s.final:
                                if k or not isinstance(i, int) or i:
                                    take_y(1 - k, k - 1, i)
                                continue
                            n = i * nb + k
                            act.wait_ge(acc_free, at(s.g + k + 1, nb, i))
                            act.wait_ge(sq_free, at(s.s + k - 1, nb, i))
                            a.activation(SQ[:, (s.s + k) % 2], X[:, n], ACT.Square).then_inc(sq_ready, 1)
                            a.activation(XH[:, n], X[:, n], ACT.Copy, scale=VEC[:, bass.ds(n + gain, 1)]).then_inc(xh_ready, 1)

                    turns = KC // s.body
                    if s.final:
                        body(0, False)
                        body(1, False)
                    with act.Fori(2 if s.final else 0, turns if s.which == "out" else turns - 1) as i:
                        body(i, False)
                    if s.which == "down":
                        body(turns - 1, True)
                    if s.final:
                        take_y(1, KC - 1, 0)
                        act.wait_ge(misc_free, s.m + KC)
                        act.dma_start(outs["y_sample"][0][:, D - P:D], YST[1][0:LS, TT]).then_inc(y_last_stored, 16)
                elif s.kind == "up":
                    def up_body(i, first, last, s=s):
                        for k in range(4):
                            if last:
                                split_hi(s.p + 4 * i + k + 2)
                            else:
                                split_hi(s.p + k + 2, 4, i)
                            if first and k == 0:
                                act.wait_ge(misc_done, s.m + 1)
                                r_scale(act, a, s.m, s.r)
                                a.preload_act_table_set("silu_and_others")
                            j = i * 2 + k // 2
                            if k % 2 == 0:
                                act.wait_ge(acc_free, at(s.g + k + 1, 4, i))
                                a.activation(TG[:], TG[:], ACT.Silu).then_inc(silu_done, 1)
                            else:
                                act.wait_ge(h_ready, at(s.j + k // 2 + 1, 2, i))
                                a.activation(HH[:, j], TU[:], ACT.Copy).then_inc(hh_ready, 1)
                    up_body(0, True, False)
                    with act.Fori(1, FC // 2 - 1) as i:
                        up_body(i, False, False)
                    up_body(FC // 2 - 1, False, True)
                    a.preload_act_table_set("natural_log_exp_and_others")

        @block.vector
        def _(dve):
            v = nc.vector
            v.memset(ONES[:], 1.0).then_inc(consts_dve, 1)
            v.memset(BLK[:], 0.0).then_inc(consts_dve, 1)
            v.memset(EPSC[:], EPS).then_inc(consts_dve, 1)
            v.memset(LG[:], 0.0).then_inc(consts_dve, 1)
            dve.wait_ge(consts_dve, 2)
            v.memset(BLK[0:FD, 0:FD], 1.0).then_inc(consts_dve, 1)
            v.memset(BLK[FD:P, FD:P], 1.0).then_inc(consts_dve, 1)
            for gi, w in enumerate(WINDOWS):
                for t in range(w - 1):
                    v.memset(INVC[:, gi, t:t + 1], 1.0 / (t + 1)).then_inc(consts_dve, 1)
            v.memset(U[:, :, 0:HIST], 0.0).then_inc(pads_ready, 1)

            def split_lo(q, per=0, i=0):
                if q >= NPANEL:
                    return
                nk, ncol = panel_shape[q]
                dve.wait_ge(hi_ready, at(q + 1, per, i))
                v.tensor_tensor(WL[:, q % SPLIT_SLOTS, 0:nk, 0:ncol], RAW[:, q % RAW_SLOTS, 0:nk, 0:ncol],
                                WH[:, q % SPLIT_SLOTS, 0:nk, 0:ncol], ALU.subtract).then_inc(lo_ready, 1)

            def split_lo_x(dst, x, gain, hi):
                return v.scalar_tensor_tensor(dst, x, gain, hi, ALU.mult, ALU.subtract)

            def sum_squares(q, width, first, acc, per=0, i=0):
                dve.wait_ge(sq_ready, at(q + 1, per, i))
                if first:
                    return v.tensor_copy(acc, SQ[:, q % 2, 0:width]).then_inc(sq_free, 1)
                dve.wait_ge(sq_free, at(q, per, i))
                return v.tensor_tensor(acc, acc, SQ[:, q % 2, 0:width], ALU.add).then_inc(sq_free, 1)

            for s in steps:
                if s.kind == "first_panel":
                    split_lo(s.p)
                elif s.kind == "group":
                    split_lo(s.p + 2)
                elif s.kind == "square" and s.g is None:
                    sum_squares(s.s, T, s.c == 0, ACC[:])
                elif s.kind == "split_x0":
                    dve.wait_ge(xh_ready, s.xs + 1)
                    split_lo_x(XL[:, s.c], X[:, s.c], VEC[:, G_MIX + s.c:G_MIX + s.c + 1], XH[:, s.c]).then_inc(xl_ready, 1)
                elif s.kind == "split_kv":
                    dve.wait_ge(yh_ready, s.ys + 1)
                    split_lo_x(HL[:, s.c], X[:, s.c], VEC[:, G_KV + s.c:G_KV + s.c + 1], HH[:, s.c]).then_inc(yl_ready, 1)
                elif s.kind == "mem_split":
                    dve.wait_ge(msq_ready, s.s + 1)
                    if s.c == 0:
                        v.tensor_copy(TG[:, 0:MT_TOK], TU[:, MSQ[s.s % 2]]).then_inc(msq_free, 1)
                    else:
                        dve.wait_ge(msq_free, s.s)
                        v.tensor_tensor(TG[:, 0:MT_TOK], TG[:, 0:MT_TOK], TU[:, MSQ[s.s % 2]], ALU.add).then_inc(msq_free, 1)
                    dve.wait_ge(mh_ready, KC * s.layer + s.c + 1)
                    vv = G_MEM + KC * s.layer + s.c
                    split_lo_x(ML[:, s.c], MTR[:, s.c], VEC[:, vv:vv + 1], MH[:, s.c]).then_inc(ml_ready, 1)
                elif s.kind == "norm":
                    dve.wait_ge(inv_ready, s.n + 1)
                    gain = {"q": GQ[:, s.layer:s.layer + 1], "fq": GQ[:, 2:3],
                            "mk": VEC[:, KN_M + s.layer:KN_M + s.layer + 1], "fk": VEC[:, KN_F:KN_F + 1]}[s.gain]
                    b = BUF[s.buf][:, s.c]
                    if s.n == 0:
                        dve.wait_ge(gate_act, 2)
                    v.scalar_tensor_tensor(b, b, gain, SQ[:, s.s % 2, 0:s.width], ALU.mult, ALU.mult).then_inc(sq_free, 1)
                elif s.kind == "evac":
                    evac(s, dve, v)
                elif s.kind == "windows":
                    windows(s, dve, v)
                elif s.kind == "pool":
                    pool(s, dve, v)
                elif s.kind == "log_sigmoid":
                    dve.wait_ge(misc_free, s.m)
                    y = LG[:, 1]
                    v.scalar_tensor_tensor(LG[:, 2], y, -1.0, y, ALU.mult, ALU.max).then_inc(gate_steps, 1)
                    dve.wait_ge(gate_act, 3)
                    v.tensor_scalar(LG[:, 4], LG[:, 3], 1.0, None, ALU.add).then_inc(gate_steps, 1)
                    dve.wait_ge(gate_steps, 2)
                    v.scalar_tensor_tensor(LG[:, 3], LG[:, 4], -1.0, LG[:, 3], ALU.add, ALU.subtract).then_inc(gate_steps, 1)
                    v.reciprocal(LG[:, 2], LG[:, 4]).then_inc(gate_steps, 1)
                    dve.wait_ge(gate_steps, 4)
                    v.tensor_tensor(LG[:, 2], LG[:, 2], LG[:, 3], ALU.mult).then_inc(gate_steps, 1)
                    dve.wait_ge(gate_act, 4)
                    dve.wait_ge(gate_steps, 5)
                    v.tensor_tensor(LG[:, 5], LG[:, 5], LG[:, 2], ALU.subtract).then_inc(gate_steps, 1)
                    dve.wait_ge(gate_steps, 6)
                    v.scalar_tensor_tensor(LG[:, 0], y, 0.0, LG[:, 5], ALU.min, ALU.subtract).then_inc(gate_steps, 1)
                    v.memset(L3[:], 0.0).then_inc(gate_steps, 1)
                    dve.wait_ge(gate_steps, GATE_STEPS)
                    dve.wait_ge(clf_loaded, 32)
                    for j in range(3):
                        v.tensor_copy(L3[:, 0:NT, 32 * j:32 * j + FH], LG[:, 0]).then_inc(gate_steps, 1)
                        v.tensor_copy(L3[:, NT:NT + PK, 32 * j:32 * j + FH], CL[:]).then_inc(gate_steps, 1)
                elif s.kind == "cumsum":
                    dve.wait_ge(misc_free, s.m + 1)
                    n = [0]

                    def link(ins):
                        n[0] += 1
                        ins.then_inc(f_steps, 1)
                        dve.wait_ge(f_steps, n[0])
                    link(v.tensor_copy(FP[:], FT[:]))
                    link(v.tensor_tensor(FT[:], FT[:], FP[:], ALU.subtract))
                    for q0 in (32, 64):
                        link(v.tensor_copy(FP[q0:q0 + 32], FT[q0:q0 + 32]))
                    link(v.tensor_tensor(FT[64:96], FT[64:96], FP[64:96], ALU.subtract))
                    link(v.tensor_copy(FP[64:96], FT[64:96]))
                    link(v.tensor_scalar(NFP[:], FP[:], -1.0, None, ALU.mult))
                    assert n[0] == F_STEPS
                elif s.kind == "scores":
                    r = s.r
                    dve.wait_ge(scores_ready, r.u + 1)
                    if r.u >= 4:
                        dve.wait_ge(probs_normed, r.u - 3)
                        dve.wait_ge(probs_ready, r.u - 3)
                    v.tensor_reduce(STAT[0:r.nq, 0, r.u % 4:r.u % 4 + 1], MISC[0:r.nq, 0, r.u % 2, 0:r.nk],
                                    AX.X, ALU.max, negate=True).then_inc(max_ready, 1)
                    if not r.first:
                        scale_probs(rows_by_unit[r.u - 1], dve, v)
                    if r.u + 1 not in rows_by_unit or rows_by_unit[r.u + 1].first:
                        scale_probs(r, dve, v)
                elif s.kind == "branch_lo":
                    r = s.r
                    c = r.c + (HC if r.att == "mem" else 0)
                    dve.wait_ge(yh_ready, r.y + 1)
                    v.tensor_tensor(HL[:, c, 0:L], ACCP[:, r.g % 2, 0, 0:L], HH[:, c, 0:L], ALU.subtract).then_inc(half_taken, 1)
                    v.tensor_tensor(HL[:, c, L:T], ACCP[:, r.g % 2, 1, 0:LS], HH[:, c, L:T], ALU.subtract).then_inc(acc_free, 1)
                elif s.kind == "resid":
                    gain = (G_FFN + KC * s.layer) if s.which == "out" else (G_MIX + KC)

                    def body(i, last, s=s, gain=gain):
                        nb, ns = s.body, s.nsub
                        for k in range(nb):
                            for q in range(ns):
                                if last:
                                    split_lo(s.p + (nb * i + k) * ns + q + 2)
                                else:
                                    split_lo(s.p + k * ns + q + 2, nb * ns, i)
                            n = i * nb + k
                            dve.wait_ge(panel_used, at(s.p + (k + 1) * ns, nb * ns, i))
                            if s.final:
                                dve.wait_ge(misc_done, at(s.m + k - 1, nb, i))
                            for hf, (lo, hi) in enumerate(halves(T)):
                                d = TGU[k][:, lo:hi] if s.final else X[:, n, lo:hi]
                                v.tensor_tensor(d, X[:, n, lo:hi], ACCP[:, (s.g + k) % 2, hf, 0:hi - lo],
                                                ALU.add).then_inc(acc_free if hf else half_taken, 1)
                            if s.final:
                                continue
                            sum_squares(s.s + k, T, False, ACC[:], nb, i)
                            dve.wait_ge(xh_ready, at(s.xs + k + 1, nb, i))
                            split_lo_x(XL[:, n], X[:, n], VEC[:, bass.ds(n + gain, 1)], XH[:, n]).then_inc(xl_ready, 1)

                    if not s.final:
                        dve.wait_ge(misc_done, s.rjob + 1)
                        v.memset(ACC[:], 0.0).then_inc(acc_zeroed, 1)
                        dve.wait_ge(acc_zeroed, s.z + 1)
                    turns = KC // s.body
                    with dve.Fori(0, turns if s.which == "out" else turns - 1) as i:
                        body(i, False)
                    if s.which == "down":
                        body(turns - 1, True)
                elif s.kind == "up":
                    def up_body(i, first, last, s=s):
                        for k in range(4):
                            if last:
                                split_lo(s.p + 4 * i + k + 2)
                            else:
                                split_lo(s.p + k + 2, 4, i)
                            if first and k == 0:
                                dve.wait_ge(r_ready, s.r + 1)
                            j = i * 2 + k // 2
                            dve.wait_ge(panel_used, at(s.p + k + 1, 4, i))
                            dst = TG if k % 2 == 0 else TU
                            for hf, (lo, hi) in enumerate(halves(T)):
                                v.tensor_tensor(dst[:, lo:hi], ACCP[:, (s.g + k) % 2, hf, 0:hi - lo], R[:, lo:hi],
                                                ALU.mult).then_inc(acc_free if hf else half_taken, 1)
                            if k % 2:
                                dve.wait_ge(acc_free, at(s.g + k + 1, 4, i))
                                dve.wait_ge(silu_done, at(s.j + k // 2 + 1, 2, i))
                                v.tensor_tensor(TU[:], TG[:], TU[:], ALU.mult).then_inc(h_ready, 1)
                                dve.wait_ge(hh_ready, at(s.j + k // 2 + 1, 2, i))
                                v.tensor_tensor(HL[:, j], TU[:], HH[:, j], ALU.subtract).then_inc(hl_ready, 1)
                    up_body(0, True, False)
                    with dve.Fori(1, FC // 2 - 1) as i:
                        up_body(i, False, False)
                    up_body(FC // 2 - 1, False, True)

        @block.tensor
        def _(pe):
            t = nc.tensor

            def product(p, g, nk, ncol, hi, lo, width, k0, first, last, per=0, i=0, ready=None, r=None):
                pe.wait_ge(lo_ready, at(p + 1, per, i))
                q = p % SPLIT_SLOTS
                hv = halves(width)
                for k in range(nk):
                    if r is not None and k == nk - 2:
                        sum_of_squares(r)
                    if ready is not None:
                        pe.wait_ge(*ready[k])
                    for n, (w, m) in enumerate(((WH, hi), (WH, lo), (WL, hi))):
                        for b, (c0_, c1_) in enumerate(hv):
                            done = last and k == nk - 1 and n == 2
                            ins_ = t.matmul(ACCP[0:ncol, g % 2, b, 0:c1_ - c0_], w[:, q, k, 0:ncol], m[:, k0 + k, c0_:c1_],
                                            start=first and k == 0 and n == 0, stop=done)
                ins_.then_inc(panel_used, 1)

            def misc_ready(m, per=0, i=0):
                if m >= 2 or per:
                    pe.wait_ge(misc_free, at(m - 1, per, i))
                if units_before.get(m, 0):
                    pe.wait_ge(probs_ready, units_before[m])
                    pe.wait_ge(pt_ready, units_before[m])

            def turn_blocks(m, blocks):
                for k, (dst, src, n) in enumerate(blocks):
                    last = t.transpose(dst, src, IDENT[0:n, 0:n])
                last.then_inc(misc_done, 1)

            def sums(m, mat, src, width):
                hv = halves(width)
                for k, (lo, hi) in enumerate(hv):
                    last = t.matmul(MISC[:, m % 2, k, 0:hi - lo], mat[:], src[:, lo:hi], start=True, stop=True)
                last.then_inc(misc_done, 1)

            def sum_of_squares(s):
                misc_ready(s.m)
                pe.wait_ge(sq_free, s.s)
                sums(s.m, ONES, ACC, T)

            pe.wait_ge(consts, 6)
            pe.wait_ge(consts_dve, DVE_CONSTS)
            for s in steps:
                if s.kind == "group":
                    hi, lo, sem_, width = moving_of(s.moving)
                    if s.g >= 2:
                        pe.wait_ge(acc_free, s.g - 1)
                    product(s.p, s.g, KC, s.ncol, hi, lo, width, 0, True, True, r=s.r,
                            ready=[(sem_, s.xs + k + 1) for k in range(KC)] if s.first else None)
                elif s.kind == "turn":
                    misc_ready(s.m)
                    ps = MISC[:, s.m % 2]
                    if s.name == "vectors":
                        pe.wait_ge(vec_loaded, 16 * (len(VECTORS) + 4))
                        turn_blocks(s.m, [(ps[:, 0, 0:NVEC], VROW[:], NVEC)])
                    elif s.name == "x":
                        pe.wait_ge(xin_loaded[s.t], 16)
                        n = P if s.t < TT else LS
                        src = XR[:, s.t] if s.t < TT else XRS[:]
                        turn_blocks(s.m, [(ps[:, k // 4, (k % 4) * P:(k % 4) * P + n], src[:, k * P:(k + 1) * P], n) for k in range(KC)])
                    elif s.name == "mem":
                        pe.wait_ge(mem_loaded, 16 * (s.layer + 1))
                        turn_blocks(s.m, [(ps[:, k // 4, (k % 4) * P:(k % 4 + 1) * P], MRAW[:, s.t, k * P:(k + 1) * P], P) for k in range(KC)])
                    elif s.name == "hist":
                        pe.wait_ge(hist_loaded, 16)
                        turn_blocks(s.m, [(ps[:, 0, 16 * k:16 * k + HIST], HRAW[:, k * P:(k + 1) * P], HIST) for k in range(HC)])
                    elif s.name == "mk":
                        pe.wait_ge(sq_free, sq_of_norm[s.n] + 1)
                        turn_blocks(s.m, [(ps[:, 0, k * P:(k + 1) * P], MKT[:, s.c, k * P:(k + 1) * P], P) for k in range(MK)])
                    elif s.name == "mv":
                        pe.wait_ge(acc_free, s.g + 1)
                        turn_blocks(s.m, [(ps[:, 0, k * P:(k + 1) * P], TGU[s.c % 2][:, k * P:(k + 1) * P], P) for k in range(MK)])
                    elif s.name == "cmk":
                        pe.wait_ge(caches_loaded, 32 * (s.layer + 1))
                        turn_blocks(s.m, [(ps[:, h // 2, (h % 2) * 256 + k * P:(h % 2) * 256 + (k + 1) * P], CMK[:, k, h * P:(h + 1) * P], P)
                                          for h in range(HC) for k in range(MK)])
                    elif s.name == "cfk":
                        pe.wait_ge(fox_loaded, 32)
                        turn_blocks(s.m, [(ps[:, h // 2, (h % 2) * 256 + k * P:(h % 2) * 256 + (k + 1) * P], CFK[:, k, h * P:(h + 1) * P], P)
                                          for h in range(HC) for k in range(PK)])
                    elif s.name == "state":
                        blocks = []
                        for w in range(2):
                            c_ = L if w == 0 else HIST + L + LS
                            blocks += [(ps[0:HIST, w, k * P:(k + 1) * P], U[:, k, c_:c_ + HIST], P) for k in range(HC)]
                        turn_blocks(s.m, blocks)
                    elif s.name in ("fk", "fv"):
                        if s.name == "fk":
                            pe.wait_ge(sq_free, sq_of_norm[s.n] + 1)
                            src = FK[:, s.c]
                        else:
                            pe.wait_ge(acc_free, s.g + 1)
                            src = TGU[s.c % 2][:]
                        turn_blocks(s.m, [(ps[:, 0, k * P:(k + 1) * P], src[:, k * P:(k + 1) * P], P) for k in range(TT)]
                                    + [(ps[0:LS, 1, 0:P], src[:, L:T], P)])
                    elif s.name == "gate":
                        pe.wait_ge(acc_free, s.g + 1)
                        turn_blocks(s.m, [(ps[:, 0, k * FH:(k + 1) * FH], TG[0:FH, k * P:(k + 1) * P], FH) for k in range(TT)]
                                    + [(ps[0:LS, 0, TT * FH:NT * FH], TG[0:FH, L:T], FH)])
                elif s.kind == "r" and s.layer:
                    sum_of_squares(s)
                elif s.kind == "rm":
                    misc_ready(s.m)
                    pe.wait_ge(ml_ready, KC * (s.r + 1))
                    sums(s.m, ONES, TG, MT_TOK)
                elif s.kind == "norm":
                    misc_ready(s.m)
                    pe.wait_ge(sq_ready, s.s + 1)
                    sums(s.m, BLK if s.block else ONES, SQ[:, s.s % 2], s.width)
                elif s.kind == "pool":
                    pe.wait_ge(pooled_in, s.n + 1)
                    pe.wait_ge(wp_loaded, 16)
                    misc_ready(s.m)
                    sums(s.m, WP[:, s.c], PD[:, s.n % 2], T)
                elif s.kind == "cumsum":
                    misc_ready(s.m)
                    pe.wait_ge(gate_steps, GATE_STEPS + 6)
                    pe.wait_ge(sel_ready, 6)
                    for k in range(TT):
                        t.matmul(MISC[0:96, s.m % 2, 0, k * P:L], L3[:, k], TRI[:, 0:L - k * P], start=k == 0, stop=k == TT - 1)
                    n = PAST + LS
                    for k in range(PK):
                        t.matmul(MISC[0:96, s.m % 2, 1, k * P:n], L3[:, NT + k], TRI[:, 0:n - k * P], start=k == 0, stop=False)
                    t.matmul(MISC[0:96, s.m % 2, 1, PAST:n], L3[0:LS, TT], TRI[0:LS, 0:LS], start=False, stop=True).then_inc(misc_done, 1)
                elif s.kind == "scores":
                    r = s.r
                    if r.first:
                        pe.wait_ge(misc_free, jobs_before[r.u])
                        pe.wait_ge(sq_free, sq_before[r.u])
                        if r.layer == 1:
                            pe.wait_ge(f_steps, F_STEPS)
                    if r.u >= 2:
                        pe.wait_ge(probs_ready, r.u - 1)
                    q0 = r.t * P
                    S = MISC[0:r.nq, 0, r.u % 2]
                    if r.att == "mem":
                        kt = MKT if r.t < TT else CMKT
                        last = t.matmul(S[:, 0:r.nk], ZQ[:, r.h, q0:q0 + r.nq], kt[:, r.h], start=True, stop=True)
                    else:
                        rows = slice(r.e * FD, (r.e + 1) * FD)
                        q = FQ[rows, r.c, q0:q0 + r.nq]
                        if r.t < TT:
                            t.matmul(S[:, 0:r.nk], q, FK[rows, r.c, 0:r.nk], start=True, stop=False)
                            f0 = 0
                        else:
                            t.matmul(S[:, 0:PAST], q, CFKT[rows, r.c], start=True, stop=False)
                            t.matmul(S[:, PAST:PAST + LS], q, FK[rows, r.c, L:T], start=False, stop=False)
                            f0 = L
                        fq = r.t * P if r.t < TT else L + PAST
                        for k in range(0, r.nk, P):
                            n = min(P, r.nk - k)
                            t.matmul(S[:, k:k + n], FP[:, fq:fq + r.nq], SEL[:, r.h, 0:n], start=False, stop=False)
                        t.matmul(S[:, 0:r.nk], SEL[:, r.h, 0:r.nq], NFP[:, f0:f0 + r.nk], start=False, stop=False)
                        last = t.matmul(S[:, r.nk - r.nq:r.nk], IDB[:, 0:r.nq], MASK[:, 0:r.nq], start=False, stop=True)
                    last.then_inc(scores_ready, 1)
                elif s.kind == "turn_probs":
                    r = s.r
                    pe.wait_ge(probs_normed, r.u + 1)
                    if r.u >= 2:
                        pe.wait_ge(pt_ready, r.u - 1)
                    for k in range(0, r.nk, P):
                        n = min(P, r.nk - k)
                        last = t.transpose(MISC[0:n, 1, r.u % 2, k:k + r.nq], PR[0:r.nq, r.u % 3, k:k + n], IDENT[0:r.nq, 0:r.nq])
                    last.then_inc(probs_turned, 1)
                elif s.kind == "values":
                    r = s.r
                    pe.wait_ge(pt_ready, r.u + 1)
                    if r.t == 0 and r.e == 0:
                        pe.wait_ge(acc_free, r.g - 1)
                    if r.att == "mem":
                        vt = MV if r.t < TT else CMV
                        tiles = [(vt[:, k, r.h * P:(r.h + 1) * P], P) for k in range(MK)]
                        rows = slice(0, P)
                    else:
                        cols = slice(r.h * FD, (r.h + 1) * FD)
                        if r.t < TT:
                            tiles = [(VT[:, k, cols], P) for k in range(r.t + 1)]
                        else:
                            tiles = [(CFV[:, k, cols], P) for k in range(PK)] + [(VT[0:LS, TT, cols], LS)]
                        rows = slice(r.e * FD, (r.e + 1) * FD)
                    o = ACCP[rows, r.g % 2, 0, r.t * P:(r.t + 1) * P] if r.t < TT else ACCP[rows, r.g % 2, 1, 0:LS]
                    for k, (vk, n) in enumerate(tiles):
                        last = t.matmul(o, vk, PT[0:n, r.u % 2, k * P:k * P + r.nq], start=k == 0, stop=k == len(tiles) - 1)
                    last.then_inc(pv_done, 1)
                elif s.kind == "resid":
                    if s.which == "down":
                        ready = [(hl_ready, s.layer * FC + k + 1) for k in range(FC)]
                    else:
                        ready = [(yl_pooled, k + 1) if s.layer == 0 and k < HC else (acc_free, branch_acc[s.layer, k] + 1)
                                 for k in range(KC)]

                    def y_turn(k, turn_, i, s=s):
                        m = s.m + turn_
                        misc_ready(m, s.body, i)
                        pe.wait_ge(acc_free, at(s.g + turn_ + 1, s.body, i))
                        ps = MISC[:, m % 2]
                        turn_blocks(m, [(ps[:, 0, b * P:(b + 1) * P], TGU[k][:, b * P:(b + 1) * P], P) for b in range(TT)]
                                    + [(ps[0:LS, 1, 0:P], TGU[k][:, L:T], P)])

                    def body(i, first, s=s, ready=ready):
                        nb, ns = s.body, s.nsub
                        for k in range(nb):
                            pe.wait_ge(acc_free, at(s.g + k - 1, nb, i))
                            for q in range(ns):
                                nk = KC if ns == 1 else SUB[q]
                                k0 = 0 if ns == 1 else SUB0[q]
                                product(s.p + k * ns + q, s.g + k, nk, P, HH, HL, T, k0, q == 0, q == ns - 1,
                                        nb * ns, i, ready[k0:k0 + nk] if first and k == 0 else None)
                            if s.final and (k or not first):
                                y_turn(1 - k, k - 1, i)

                    body(0, True)
                    with pe.Fori(1, KC // s.body) as i:
                        body(i, False)
                    if s.final:
                        y_turn(1, KC - 1, 0)
                elif s.kind == "up":
                    def up_body(i, first, s=s):
                        for k in range(4):
                            pe.wait_ge(acc_free, at(s.g + k - 1, 4, i))
                            product(s.p + k, s.g + k, KC, P, XH, XL, T, 0, True, True, 4, i,
                                    [(xl_ready, s.xs + c + 1) for c in range(KC)] if first and k == 0 else None)
                            if first and k == 0:
                                misc_ready(s.m)
                                pe.wait_ge(sq_free, s.s)
                                sums(s.m, ONES, ACC, T)
                    up_body(0, True)
                    with pe.Fori(1, FC // 2) as i:
                        up_body(i, False)


_INS = ["x_prompt", "x_sample", "state_pool", "cache_fox_k", "cache_fox_v", "cache_fox_logf", "cache_mem_k",
        "cache_mem_v", "mem_prompt", "g_mix", "w_in", "w_out", "q_norm_mem", "g_mem", "w_mem_kv", "k_norm_mem",
        "w_pool", "pool_scale", "q_norm_fox", "g_kv", "w_kv", "k_norm_fox", "b_f", "g_ffn", "w_gu", "w_down"]


def kernel(**inputs):
    import concourse.bacc as bacc
    from concourse.bass_utils import run_bass_kernel_spmd

    B, L, D = inputs["x_prompt"].shape
    DB, LS, _ = inputs["x_sample"].shape
    NA, _, HIST, PW = inputs["state_pool"].shape
    _, _, FH, FD = inputs["cache_fox_k"].shape
    DEPTH, _, M, MHEADS, MD = inputs["cache_mem_k"].shape
    shapes = {
        "y_prompt": (B, L, D), "y_sample": (DB, LS, D), "pool_state_prompt": (NA, B, HIST, PW),
        "fox_k_prompt": (B, L, FH, FD), "fox_v_prompt": (B, L, FH, FD), "fox_logf_prompt": (B, L, FH),
        "mem_k_prompt": (DEPTH, B, M, MHEADS, MD), "mem_v_prompt": (DEPTH, B, M, MHEADS, MD),
        "pool_state_sample": (NA, DB, HIST, PW),
        "fox_k_sample": (DB, LS, FH, FD), "fox_v_sample": (DB, LS, FH, FD), "fox_logf_sample": (DB, LS, FH),
    }
    nc = bacc.Bacc("TRN2", target_bir_lowering=False, num_devices=1)
    arrays, ins = {}, {}
    for name in _INS:
        a = np.ascontiguousarray(inputs[name])
        arrays[f"in_{name}"] = a
        ins[name] = nc.dram_tensor(f"in_{name}", a.shape, mybir.dt.from_np(a.dtype), kind="ExternalInput").ap()
    outs = {name: nc.dram_tensor(f"out_{name}", shape, F32, kind="ExternalOutput").ap() for name, shape in shapes.items()}
    encoder_kernel(nc, ins, outs)
    r = run_bass_kernel_spmd(nc, [arrays], core_ids=[0])
    return tuple(r.results[0][f"out_{name}"] for name in shapes)
```
